# Optimizing a Trainium2 kernel written in Bass

```python
import math
import jax, jax.numpy as jnp
from jax import lax
import numpy as np

D_MODEL = 2048
BATCH = 1
SEQ = 256
DEPTH = 1

HEAD_DIM = 128
A_HEADS = 8
A_WIDTH = A_HEADS * HEAD_DIM
IDX_HEADS = 16
IDX_DIM = 64
TOPK_MAX = 256
B_HEADS = 4
B_WIDTH = B_HEADS * 2 * HEAD_DIM
Q_BLOCK = 128
ROPE_THETA = 10000.0
NORM_EPS = 1e-6
SUBLN_EPS = 1e-5

SPLIT_SIZES = (
    A_WIDTH, A_WIDTH, A_WIDTH, A_WIDTH,
    IDX_HEADS * IDX_DIM, IDX_DIM, IDX_HEADS,
    B_WIDTH, B_WIDTH, B_WIDTH, B_WIDTH,
    D_MODEL, D_MODEL,
)
IN_COLS = sum(SPLIT_SIZES)

kernel_name = 'hybrid_dsa_diffattn_gated_merge'

def rms_norm(x, gain, eps=NORM_EPS):
    xf = x.astype(jnp.float32)
    y = xf * lax.rsqrt(jnp.mean(xf * xf, axis=-1, keepdims=True) + eps)
    return (y * gain.astype(jnp.float32)).astype(x.dtype)

def rope_tables(positions, dim):
    inv_freq = ROPE_THETA ** (-jnp.arange(0, dim, 2, dtype=jnp.float32) / dim)
    ang = positions.astype(jnp.float32)[..., None] * inv_freq
    return jnp.cos(ang), jnp.sin(ang)

def apply_rope(x, cos, sin):
    shape = cos.shape[:2] + (1,) * (x.ndim - 3) + cos.shape[-1:]
    c = cos.reshape(shape).astype(x.dtype)
    s = sin.reshape(shape).astype(x.dtype)
    x1, x2 = jnp.split(x, 2, axis=-1)
    return jnp.concatenate([x1 * c - x2 * s, x2 * c + x1 * s], axis=-1)

def setup_inputs(seed: int = 0) -> dict:
    key = jax.random.key(seed)
    ks = jax.random.split(key, 16)
    f32 = jnp.float32
    x = jax.random.normal(ks[0], (BATCH, SEQ, D_MODEL), f32)
    positions = jnp.broadcast_to(jnp.arange(SEQ, dtype=jnp.int32), (BATCH, SEQ))
    norm_gain = 1.0 + 0.02 * jax.random.normal(ks[1], (DEPTH, D_MODEL), f32)
    w_in = jax.random.normal(ks[2], (DEPTH, D_MODEL, IN_COLS), f32) * D_MODEL ** -0.5
    a_q_gain = 1.0 + 0.02 * jax.random.normal(ks[3], (DEPTH, HEAD_DIM), f32)
    a_k_gain = 1.0 + 0.02 * jax.random.normal(ks[4], (DEPTH, HEAD_DIM), f32)
    b_q_gain = 1.0 + 0.02 * jax.random.normal(ks[5], (DEPTH, HEAD_DIM), f32)
    b_k_gain = 1.0 + 0.02 * jax.random.normal(ks[6], (DEPTH, HEAD_DIM), f32)
    lambda_q1 = 0.1 * jax.random.normal(ks[7], (DEPTH, HEAD_DIM), f32)
    lambda_k1 = 0.1 * jax.random.normal(ks[8], (DEPTH, HEAD_DIM), f32)
    lambda_q2 = 0.1 * jax.random.normal(ks[9], (DEPTH, HEAD_DIM), f32)
    lambda_k2 = 0.1 * jax.random.normal(ks[10], (DEPTH, HEAD_DIM), f32)
    b_subln_gain = 1.0 + 0.02 * jax.random.normal(ks[11], (DEPTH, 2 * HEAD_DIM), f32)
    w_o_a = jax.random.normal(ks[12], (DEPTH, A_WIDTH, D_MODEL), f32) * A_WIDTH ** -0.5
    w_o_b = jax.random.normal(ks[13], (DEPTH, B_WIDTH, D_MODEL), f32) * B_WIDTH ** -0.5
    w_out = jax.random.normal(ks[14], (DEPTH, D_MODEL, D_MODEL), f32) * D_MODEL ** -0.5
    return {'x': x, 'positions': positions, 'norm_gain': norm_gain, 'w_in': w_in,
            'a_q_gain': a_q_gain, 'a_k_gain': a_k_gain, 'b_q_gain': b_q_gain, 'b_k_gain': b_k_gain,
            'lambda_q1': lambda_q1, 'lambda_k1': lambda_k1, 'lambda_q2': lambda_q2, 'lambda_k2': lambda_k2,
            'b_subln_gain': b_subln_gain, 'w_o_a': w_o_a, 'w_o_b': w_o_b, 'w_out': w_out}

def reference(x, positions, norm_gain, w_in, a_q_gain, a_k_gain, b_q_gain, b_k_gain,
              lambda_q1, lambda_k1, lambda_q2, lambda_k2, b_subln_gain, w_o_a, w_o_b, w_out):
    B, S, _ = x.shape
    nb = S // Q_BLOCK
    topk = min(TOPK_MAX, S // 4)
    offsets = np.cumsum(SPLIT_SIZES)[:-1].tolist()
    cos_h, sin_h = rope_tables(positions, HEAD_DIM)
    cos_i, sin_i = rope_tables(positions, IDX_DIM)
    key_idx = jnp.arange(S)
    q_idx_blocks = jnp.arange(S).reshape(nb, Q_BLOCK)

    def to_blocks(t):
        return jnp.swapaxes(t.reshape((B, nb, Q_BLOCK) + t.shape[2:]), 0, 1)

    def from_blocks(t):
        return jnp.swapaxes(t, 0, 1).reshape((B, S) + t.shape[3:])

    for l in range(DEPTH):
        h = rms_norm(x, norm_gain[l])
        proj = jnp.einsum('bsd,dn->bsn', h, w_in[l])
        (qa, ka, va, ga, qi, ki, wi, qb, kb, vb, gb, ma, mb) = jnp.split(proj, offsets, axis=-1)

        qa = apply_rope(rms_norm(qa.reshape(B, S, A_HEADS, HEAD_DIM), a_q_gain[l]), cos_h, sin_h)
        ka = apply_rope(rms_norm(ka.reshape(B, S, A_HEADS, HEAD_DIM), a_k_gain[l]), cos_h, sin_h)
        va = va.reshape(B, S, A_HEADS, HEAD_DIM)
        qi = apply_rope(qi.reshape(B, S, IDX_HEADS, IDX_DIM), cos_i, sin_i)
        ki = apply_rope(ki, cos_i, sin_i)
        wi = wi * (IDX_HEADS ** -0.5 * IDX_DIM ** -0.5)

        def a_block(args):
            qa_b, qi_b, wi_b, t_b = args
            rel = jax.nn.relu(jnp.einsum('bqhd,bsd->bqhs', qi_b, ki).astype(jnp.float32))
            score = jnp.einsum('bqhs,bqh->bqs', rel, wi_b.astype(jnp.float32))
            causal = key_idx[None, :] <= t_b[:, None]
            score = jnp.where(causal[None], score, -jnp.inf)
            _, sel = lax.top_k(score, topk)
            k_sel = jax.vmap(lambda kk, ii: kk[ii])(ka, sel)
            v_sel = jax.vmap(lambda vv, ii: vv[ii])(va, sel)
            s = jnp.einsum('bqhd,bqkhd->bqhk', qa_b, k_sel).astype(jnp.float32) * HEAD_DIM ** -0.5
            valid = (sel <= t_b[None, :, None])[:, :, None, :]
            p = jax.nn.softmax(jnp.where(valid, s, -jnp.inf), axis=-1)
            return jnp.einsum('bqhk,bqkhd->bqhd', p.astype(v_sel.dtype), v_sel)

        oa = lax.map(a_block, (to_blocks(qa), to_blocks(qi), to_blocks(wi), q_idx_blocks))
        oa = from_blocks(oa).reshape(B, S, A_WIDTH)

        lambda_init = 0.8 - 0.6 * math.exp(-0.3 * l)
        lam = (jnp.exp(jnp.sum(lambda_q1[l].astype(jnp.float32) * lambda_k1[l].astype(jnp.float32)))
               - jnp.exp(jnp.sum(lambda_q2[l].astype(jnp.float32) * lambda_k2[l].astype(jnp.float32)))
               + lambda_init)
        qb = apply_rope(rms_norm(qb.reshape(B, S, B_HEADS, 2, HEAD_DIM), b_q_gain[l]), cos_h, sin_h)
        kb = apply_rope(rms_norm(kb.reshape(B, S, B_HEADS, 2, HEAD_DIM), b_k_gain[l]), cos_h, sin_h)
        vb = vb.reshape(B, S, B_HEADS, 2 * HEAD_DIM)

        def b_block(args):
            q_b, t_b = args
            s = jnp.einsum('bqhcd,bshcd->bhcqs', q_b, kb).astype(jnp.float32) * HEAD_DIM ** -0.5
            causal = key_idx[None, :] <= t_b[:, None]
            p = jax.nn.softmax(jnp.where(causal[None, None, None], s, -jnp.inf), axis=-1)
            attn = p[:, :, 0] - lam * p[:, :, 1]
            return jnp.einsum('bhqs,bshe->bqhe', attn.astype(vb.dtype), vb)

        ob = from_blocks(lax.map(b_block, (to_blocks(qb), q_idx_blocks)))
        ob = (rms_norm(ob, b_subln_gain[l], SUBLN_EPS) * (1.0 - lambda_init)).reshape(B, S, B_WIDTH)

        ya = jnp.einsum('bsc,cd->bsd', oa * jax.nn.silu(ga), w_o_a[l])
        yb = jnp.einsum('bsc,cd->bsd', ob * jax.nn.silu(gb), w_o_b[l])
        merged = jax.nn.sigmoid(ma) * ya + jax.nn.sigmoid(mb) * yb
        x = x + jnp.einsum('bsd,de->bse', merged, w_out[l])
    return x


_drawn_inputs = setup_inputs


def setup_inputs(seed=0):
    import zlib

    import numpy as np

    out = dict(_drawn_inputs(seed))
    spreads = {}
    factors = {'norm_gain': 4.18,
     'a_q_gain': 8.0,
     'a_k_gain': 8.0,
     'b_q_gain': 8.0,
     'b_k_gain': 8.0,
     'lambda_k1': 57.728,
     'lambda_q2': 7.039,
     'lambda_k2': 4.773,
     'b_subln_gain': 27.199,
     'lambda_q1': 8.0}
    for name, (base, spread) in spreads.items():
        noise = np.random.default_rng([zlib.crc32(name.encode()), seed]).standard_normal(out[name].shape)
        drawn = base * np.exp(spread * noise) if base else spread * noise
        out[name] = __import__('jax').numpy.asarray(drawn.astype(out[name].dtype))
    for name, factor in factors.items():
        out[name] = (out[name] * factor).astype(out[name].dtype)
    return out
```

```python
from contextlib import ExitStack

import concourse.bass as bass
from concourse import mybir
from concourse.alu_op_type import AluOpType as ALU

ACT = mybir.ActivationFunctionType
F32 = mybir.dt.float32
F32R = mybir.dt.float32r
I32 = mybir.dt.int32

P = 128
D = 2048
S = 256
RT = S // P
KT = D // P
HD = 128
IDX_HEADS, IDX_DIM = 16, 64
TOPK = S // 4
A_HEADS, B_HEADS = 8, 4
NORM_EPS, SUBLN_EPS = 1e-6, 1e-5
LAMBDA_INIT = 0.2
SCALE = HD ** -0.5
IDX_SCALE = IDX_HEADS ** -0.5 * IDX_DIM ** -0.5

CW = 512
CK = 8
RING = 4
KIWI = IDX_DIM + IDX_HEADS
A_W = A_HEADS * HD

COL = {}
_at = 0
for _name, _width in (("qa", A_W), ("ka", A_W), ("va", A_W), ("ga", A_W), ("qi", A_W), ("kiwi", KIWI),
                      ("qb", A_W), ("kb", A_W), ("vb", A_W), ("gb", A_W), ("ma", D), ("mb", D)):
    COL[_name] = _at
    _at += _width
IN_COLS = _at

C_QI, C_QK, C_V, C_G, C_M = 0, 2, 10, 14, 18
C_O = 26
U_O = C_O * CK
U_W = U_O + 8 * 4
U_END = U_W + 4 * CK
C_INDEX = 11
U_TOPK = 15 * CK
U_A = 16 * CK
U_B = U_A + 4 * A_HEADS
U_OGT = U_B + 8 * B_HEADS
U_KIWI = 16

NEG = -1.0e30
MARK = -3.0e38
TWO_PI_1 = 6.28125
TWO_PI_2 = 0.0019350051879882812
TWO_PI_3 = 3.0199159819e-07
ROUND = 12582912.0
PI_BELOW = 3.1415925
HALF_PI = 1.5707963267948966


def build_layer(nc, x, positions, inv_freq, norm_gain, w_in, a_q_gain, a_k_gain, b_q_gain, b_k_gain,
                lambda_q1, lambda_k1, lambda_q2, lambda_k2, b_subln_gain, w_o_a, w_o_b, w_out, out):
    x_rows = x[0].rearrange("(r p) d -> p r d", p=P)
    out_rows = out[0].rearrange("(r p) d -> p r d", p=P)

    with ExitStack() as ctx:
        place = [-(-nc.sbuf_base // 64) * 64]

        def sb(name, shape, dt=F32, at=None):
            size = 4
            for n in shape[1:]:
                size *= n
            offset = place[0] if at is None else at
            if at is None:
                place[0] += -(-size // 64) * 64
                assert place[0] <= nc.sbuf_usable_end, (name, place[0])
            return nc.alloc_sbuf_tensor_at(name, shape, dt, offset=offset)

        def sem(name):
            return ctx.enter_context(nc.semaphore(name))

        raw = sb("raw", [P, RING, 2, CW])
        hi = sb("hi", [P, RING, 2, CW], F32R)
        lo = sb("lo", [P, RING, 2, CW], F32R)
        hT_hi = sb("hT_hi", [P, KT, S], F32R)
        hT_lo = sb("hT_lo", [P, KT, S], F32R)
        qk_at = place[0]
        qkT = sb("qkT", [P, 5 * 8, S])
        ogT_hi = sb("ogT_hi", [P, KT, S], F32R, at=qk_at)
        ogT_lo = sb("ogT_lo", [P, KT, S], F32R, at=qk_at + 4 * KT * S)
        QI, QA, KA, QB, KB = 0, 8, 16, 24, 32
        v = sb("v", [P, RT, 2 * A_W])
        g = sb("g", [P, RT, 2 * A_W])
        m_at = place[0]
        m = sb("m", [P, RT, 2 * D])
        xr = m[:, 0, :].rearrange("p (r d) -> p r d", r=RT)
        kiwi_raw = m[:, 1, 0:KT * KIWI].rearrange("p (k n) -> p k n", k=KT)
        kiwi_hi = sb("kiwi_hi", [P, KT, KIWI], F32R, at=m_at + 4 * (2 * D + KT * KIWI))
        kiwi_lo = sb("kiwi_lo", [P, KT, KIWI], F32R, at=m_at + 4 * (2 * D + 2 * KT * KIWI))

        ident = sb("ident", [P, P])
        stage = sb("stage", [P, RT, CW])
        roped = sb("roped", [P, RT, CW])
        swapped = sb("swapped", [P, RT, CW])
        QB_COLS = 3 * P
        work_flat = [stage[:, :, :].rearrange("p r n -> p (r n)"),
                     roped[:, :, :].rearrange("p r n -> p (r n)"),
                     swapped[:, :, :].rearrange("p r n -> p (r n)")]
        masked = [work_flat[0][:, i * QB_COLS:(i + 1) * QB_COLS] for i in range(2)]
        probs = [work_flat[1][:, i * QB_COLS:(i + 1) * QB_COLS] for i in range(2)]
        probsT = [work_flat[2][:, i * QB_COLS:(i + 1) * QB_COLS] for i in range(2)]
        rel = masked
        score = sb("score", [P, QB_COLS])
        bias_a = sb("bias_a", [P, QB_COLS])
        bias_b = sb("bias_b", [P, QB_COLS])
        kiT = sb("kiT", [P, S])
        w_idx = sb("w_idx", [P, RT, IDX_HEADS])
        sub_gain = sb("sub_gain", [P, 2 * HD])
        gain_rows = sb("gain_rows", [KT, P])
        gainT = sb("gainT", [P, KT])
        top8 = sb("top8", [P, 2, 8])
        pos_i = sb("pos_i", [P, RT], I32)
        pos_f = sb("pos_f", [P, RT])
        half = sb("half", [P, 8])
        small = sb("small", [P, 96])
        ss_x, ms_x, rstd = small[:, 0:2], small[:, 2:4], small[:, 4:6]
        ss_h, ms_h, r_h = small[:, 8:16], small[:, 16:24], small[:, 24:32]
        lam_s, lam_e, neg_lam = small[:, 32:34], small[:, 34:36], small[:, 36:37]
        max_s, neg_max, sum_p = small[:, 40:44], small[:, 44:48], small[:, 48:52]
        inv_p, mix = small[:, 52:56], small[:, 56:58]
        ss_o, ms_o, r_o, f_o = small[:, 60:62], small[:, 62:64], small[:, 64:66], small[:, 66:68]

        v0 = v[:, 0, :]
        gains = v0[:, 0:512].rearrange("p (i d) -> p i d", i=4)
        lams = v0[:, 512:1024].rearrange("p (i d) -> p i d", i=4)
        lam_prod = v0[:, 1024:1280].rearrange("p (i d) -> p i d", i=2)
        v1 = v[:, 1, :]
        freq = v1[:, 0:64]

        def phases(n):
            return v1[:, 64 + 128 * n:192 + 128 * n]

        ang, turns, red1, red2, red3, red4, absr, sin_t, cos_t, nsin_t = (phases(n) for n in range(10))
        kst = v1[:, 1408:1568].rearrange("p (r n) -> p r n", r=RT)
        k_cos = v1[:, 1568:1696].rearrange("p (r n) -> p r n", r=RT)
        k_swap = v1[:, 1696:1824].rearrange("p (r n) -> p r n", r=RT)
        kr = v0[:, 1280:1536].rearrange("p (r n) -> p r n", r=RT)
        tab_c = g[:, 0, 0:1024].rearrange("p (i r d) -> p i r d", i=4, r=RT)
        tab_s = g[:, 0, 1024:2048].rearrange("p (i r d) -> p i r d", i=4, r=RT)
        tab_ci = g[:, 1, 0:128].rearrange("p (r d) -> p r d", r=RT)
        tab_si = g[:, 1, 128:256].rearrange("p (r d) -> p r d", r=RT)

        ps = ctx.enter_context(nc.psum_tensor("ps", [P, 8, CW], F32))
        T0, S0 = 4, 6

        x_landed = [sem(f"x_landed_{i}") for i in range(4)]
        consts_landed = sem("consts_landed")
        gain_landed = sem("gain_landed")
        kiwi_landed = sem("kiwi_landed")
        raw_landed = [sem(f"raw_landed_{i}") for i in range(RING)]
        res_landed = sem("res_landed")
        out_landed = sem("out_landed")
        ident_ready = sem("ident_ready")
        causal_ready = sem("causal_ready")
        pool_wrote = sem("pool_wrote")
        hi_ready, lo_ready, unit_done = sem("hi_ready"), sem("lo_ready"), sem("unit_done")
        kiwi_hi_ready, kiwi_lo_ready, kiwi_done = sem("kiwi_hi_ready"), sem("kiwi_lo_ready"), sem("kiwi_done")
        chunk_out, tail_out = sem("chunk_out"), sem("tail_out")
        split_T, split_hi, split_lo = sem("split_T"), sem("split_hi"), sem("split_lo")
        gainT_psum, gainT_ready = sem("gainT_psum"), sem("gainT_ready")
        reduced, sin_ready = sem("reduced"), sem("sin_ready")
        lam_exps = sem("lam_exps")
        x_squares, rstd_ready = sem("x_squares"), sem("rstd_ready")
        h_squares, r_h_ready, rope_done = sem("h_squares"), sem("r_h_ready"), sem("rope_done")
        qk_transposed, qkT_ready = sem("qk_transposed"), sem("qkT_ready")
        kiwi_out, ki_roped, ki_transposed, kiT_ready = (sem("kiwi_out"), sem("ki_roped"),
                                                        sem("ki_transposed"), sem("kiT_ready"))
        idx_scores, idx_relu, idx_added = sem("idx_scores"), sem("idx_relu"), sem("idx_added")
        scores, neg_max_ready, probs_ready = sem("scores"), sem("neg_max_ready"), sem("probs_ready")
        probsT_psum, probsT_ready, heads_psum, og_ready = (sem("probsT_psum"), sem("probsT_ready"),
                                                           sem("heads_psum"), sem("og_ready"))
        mixed = sem("mixed")
        o_squares, r_o_ready = sem("o_squares"), sem("r_o_ready")
        gates_ready = sem("gates_ready")
        merged = sem("merged")
        last_rows = sem("last_rows")
        dve_wrote, act_wrote = sem("dve_wrote"), sem("act_wrote")

        block = ctx.enter_context(nc.Block())

        @block.sync
        def _(sp):
            def load_x(j):
                sp.dma_start(xr[:, :, j * CW:(j + 1) * CW],
                             x_rows[:, :, j * CW:(j + 1) * CW]).then_inc(x_landed[j], 16)

            def load(slot, u, weights, k0, col):
                if not isinstance(u, int) or u >= RING:
                    sp.wait_ge(lo_ready, u - (RING - 1))
                src = weights[0][k0 * P:(k0 + 2) * P, bass.ds(col, CW)].rearrange("(k p) n -> p k n", p=P)
                sp.dma_start(raw[:, slot], src).then_inc(raw_landed[slot], 16)

            def load_chunk(c, col):
                for i in range(CK):
                    load(i % RING, c * CK + i, w_in, 2 * i, col)

            for i in range(CK):
                if i in (0, 2):
                    load_x(i // 2)
                if i == 4:
                    load_x(2)
                    load_x(3)
                    sp.dma_start(pos_i[:, :], positions[0].rearrange("(r p) -> p r", p=P),
                                  allow_slow_non_contiguous=True).then_inc(consts_landed, 16)
                    sp.dma_start(freq, inv_freq[0].partition_broadcast(P)).then_inc(consts_landed, 16)
                    for j, row in enumerate((a_q_gain, a_k_gain, b_q_gain, b_k_gain)):
                        sp.dma_start(gains[:, j], row[0].partition_broadcast(P)).then_inc(consts_landed, 16)
                    for j, row in enumerate((lambda_q1, lambda_k1, lambda_q2, lambda_k2)):
                        sp.dma_start(lams[:, j], row[0].partition_broadcast(P)).then_inc(consts_landed, 16)
                    sp.dma_start(sub_gain[:, :], b_subln_gain[0].partition_broadcast(P)).then_inc(consts_landed, 16)
                load(i % RING, i, w_in, 2 * i, COL["qi"])
            for i in range(CK):
                if i in (2, 5):
                    k = KT // 2 * (i // 5)
                    sp.dma_start(kiwi_raw[:, k:k + KT // 2],
                                 w_in[0][k * P:(k + KT // 2) * P, COL["kiwi"]:COL["kiwi"] + KIWI]
                                 .rearrange("(k p) n -> p k n", p=P)).then_inc(kiwi_landed, 16)
                load(i % RING, CK + i, w_in, 2 * i, COL["qi"] + CW)
            with sp.Fori(0, 2) as branch:
                with sp.Fori(0, 4) as n:
                    load_chunk(C_QK + branch * 4 + n, branch * COL["qb"] + n * CW)
            for c, name in ((C_V, "va"), (C_V + 2, "vb"), (C_G, "ga"), (C_G + 2, "gb")):
                with sp.Fori(0, 2) as n:
                    load_chunk(n + c, n * CW + COL[name])
            with sp.Fori(0, 8) as n:
                load_chunk(n + C_M, n * CW + COL["ma"])
            for n in range(4):
                for b, weights in enumerate((w_o_a, w_o_b)):
                    for i in range(4):
                        load(i, U_O + 8 * n + 4 * b + i, weights, 2 * i, n * CW)
                if n == 0:
                    sp.wait_ge(split_lo, 16)
                    sp.dma_start(g[:, :, :], x_rows).then_inc(res_landed, 16)
            for n in range(4):
                for i in range(CK):
                    load(i % RING, U_W + CK * n + i, w_out, 2 * i, n * CW)
            for n in range(3):
                sp.wait_ge(tail_out, 8 + n + 1)
                sp.dma_start(out_rows[:, :, n * CW:(n + 1) * CW],
                             g[:, :, n * CW:(n + 1) * CW]).then_inc(out_landed, 16)
            for r in range(RT):
                sp.wait_ge(tail_out, 11 + r + 1)
                sp.dma_start(out_rows[:, r, 3 * CW:4 * CW], g[:, r, 3 * CW:4 * CW]).then_inc(out_landed, 16)
            sp.wait_ge(out_landed, 5 * 16)

        @block.gpsimd
        def _(pool):
            nc.gpsimd.memset(ident[:, :], 0.0).then_inc(pool_wrote, 1)
            nc.gpsimd.memset(bias_b[:, :], 0.0).then_inc(pool_wrote, 1)
            nc.gpsimd.memset(half[:, :], -0.5).then_inc(pool_wrote, 1)
            pool.wait_ge(pool_wrote, 3)
            nc.gpsimd.affine_select(out=ident[:, :], in_=ident[:, :], compare_op=ALU.not_equal, fill=1.0,
                                    base=0, pattern=[[-1, P]], channel_multiplier=1).then_inc(ident_ready, 1)
            for start in (0, 2 * P):
                blk = bias_b[:, start:start + P]
                last = nc.gpsimd.affine_select(out=blk, in_=blk, compare_op=ALU.is_ge, fill=NEG, base=0,
                                               pattern=[[-1, P]], channel_multiplier=1)
            last.then_inc(causal_ready, 1)
            wrote = [3]

            def root(out, mean, total, n, width, eps):
                nc.gpsimd.tensor_scalar(mean, total, 1.0 / n, eps, ALU.mult, ALU.add).then_inc(pool_wrote, 1)
                wrote[0] = wrote[0] + 1
                pool.wait_ge(pool_wrote, wrote[0])
                return nc.gpsimd.tensor_tensor(out, mean, half[:, 0:width], ALU.pow)

            pool.wait_ge(x_squares, 1)
            root(rstd, ms_x, ss_x, D, RT, NORM_EPS).then_inc(rstd_ready, 1)
            for n in range(8):
                pool.wait_ge(h_squares, n + 1)
                root(r_h, ms_h, ss_h, HD, 8, NORM_EPS).then_inc(r_h_ready, 1)
            for h in range(B_HEADS):
                pool.wait_ge(o_squares, h + 1)
                root(r_o, ms_o, ss_o, 2 * HD, RT, SUBLN_EPS).then_inc(r_o_ready, 1)

        @block.tensor
        def _(pe):
            mm = nc.tensor.matmul

            def unit(u, slot, k0, s_hi, s_lo, bank, first, last, rows_done=None):
                pe.wait_ge(lo_ready, u + 1)
                order = [(j, r) for j in range(2) for r in range(RT)]
                if rows_done is not None:
                    order.sort(key=lambda jr: jr[1])
                for j, r in order:
                    a_hi = s_hi[:, k0 + j, r * P:(r + 1) * P]
                    a_lo = s_lo[:, k0 + j, r * P:(r + 1) * P]
                    o = ps[:, bank + r, :]
                    mm(o, a_hi, hi[:, slot, j], start=first and j == 0, stop=False)
                    mm(o, a_hi, lo[:, slot, j], start=False, stop=False)
                    ins = mm(o, a_lo, hi[:, slot, j], start=False, stop=last and j == 1)
                    if rows_done is not None and j == 1 and r == 0:
                        ins.then_inc(rows_done, 1)
                ins.then_inc(unit_done, 1)

            def w_in_unit(c, i, parity):
                if isinstance(c, int) and c == 0:
                    pe.wait_ge(split_lo, i + 1)
                if i == 0 and (not isinstance(c, int) or c >= 2):
                    pe.wait_ge(chunk_out, c - 1)
                unit(c * CK + i, i % RING, 2 * i, hT_hi, hT_lo, 2 * parity, i == 0, i == CK - 1)

            def transpose_roped(n):
                pe.wait_ge(rope_done, n + 1)
                if not isinstance(n, int) or n > 0:
                    pe.wait_ge(qkT_ready, n)
                for b in range(4):
                    for r in range(RT):
                        o = ps[:, T0 + b // 2, (b % 2) * S + r * P:(b % 2) * S + (r + 1) * P]
                        ins = nc.tensor.transpose(o, roped[:, r, b * P:(b + 1) * P], ident[:, :])
                ins.then_inc(qk_transposed, 1)

            def transpose_step(rows, bank):
                for b in range(2):
                    for r in range(RT):
                        o = ps[:, bank, b * S + r * P:b * S + (r + 1) * P]
                        ins = nc.tensor.transpose(o, rows(b, r), ident[:, :])
                ins.then_inc(split_T, 1)

            pe.wait_ge(ident_ready, 1)
            pe.wait_ge(gain_landed, 16)
            nc.tensor.transpose(ps[:, 0, 0:KT], gain_rows[:, :], ident[0:KT, 0:KT]).then_inc(gainT_psum, 1)

            def transpose_x(n):
                if n % 2 == 0:
                    pe.wait_ge(x_landed[n // 2], 16)
                if n >= 4:
                    pe.wait_ge(split_lo, n - 3)
                transpose_step(lambda b, r: xr[:, r, (2 * n + b) * P:(2 * n + b + 1) * P], 4 + n % 4)

            for n in range(4):
                transpose_x(n)
            pe.wait_ge(gainT_ready, 1)
            for i in range(CK):
                if i in (1, 2):
                    transpose_x(2 * i + 2)
                    transpose_x(2 * i + 3)
                w_in_unit(0, i, 0)
            for i in range(CK):
                if i == 6:
                    pe.wait_ge(split_lo, 8)
                    transpose_roped(0)
                w_in_unit(1, i, 1)

            for c in (2, 3):
                for i in range(CK):
                    if c == 2 and i == 2:
                        pe.wait_ge(kiwi_lo_ready, 1)
                        for k in range(KT):
                            for r in range(RT):
                                a_hi, a_lo = hT_hi[:, k, r * P:(r + 1) * P], hT_lo[:, k, r * P:(r + 1) * P]
                                o = ps[:, S0 + r, 0:KIWI]
                                mm(o, a_hi, kiwi_hi[:, k], start=k == 0, stop=False)
                                mm(o, a_hi, kiwi_lo[:, k], start=False, stop=False)
                                ins = mm(o, a_lo, kiwi_hi[:, k], start=False, stop=k == KT - 1)
                        ins.then_inc(kiwi_done, 1)
                    if c == 3 and i == 0:
                        pe.wait_ge(ki_roped, 1)
                        for r in range(RT):
                            ins = nc.tensor.transpose(ps[:, S0, r * P:(r + 1) * P], kr[:, r, :], ident[:, :])
                        ins.then_inc(ki_transposed, 1)
                    if i == 6:
                        transpose_roped(c - 1)
                    w_in_unit(c, i, c % 2)
            with pe.Fori(0, 3) as pair:
                for parity in range(2):
                    c = pair * 2 + (4 + parity)
                    for i in range(CK):
                        if i == 6:
                            transpose_roped(c - 1)
                        w_in_unit(c, i, parity)

            def index_scores(h):
                if h < 2:
                    pe.wait_ge(kiT_ready, 1)
                    pe.wait_ge(qkT_ready, 2)
                else:
                    pe.wait_ge(idx_relu, h - 1)
                a = (h % 2) * IDX_DIM
                q = qkT[a:a + IDX_DIM, QI + h // 2, :]
                k = kiT[a:a + IDX_DIM, :]
                o = ps[:, S0 + h % 2, :]
                mm(o[:, 0:P], q[:, 0:P], k[:, 0:P], start=True, stop=True)
                mm(o[:, P:P + S], q[:, P:S], k[:, :], start=True, stop=True).then_inc(idx_scores, 1)

            def qk_scores(q_block, k_block, bank):
                o = ps[:, bank, :]
                mm(o[:, 0:P], qkT[:, q_block, 0:P], qkT[:, k_block, 0:P], start=True, stop=True)
                mm(o[:, P:P + S], qkT[:, q_block, P:S], qkT[:, k_block, :],
                   start=True, stop=True).then_inc(scores, 1)

            def transpose_probs(src, head):
                for b in range(3):
                    ins = nc.tensor.transpose(ps[:, T0 + head % 2, b * P:(b + 1) * P],
                                              src[:, b * P:(b + 1) * P], ident[:, :])
                ins.then_inc(probsT_psum, 1)

            def weighted_values(pT, bank, col, width):
                o = ps[:, bank, :]
                mm(o[:, 0:width], pT[:, 0:P], v[:, 0, col:col + width], start=True, stop=True)
                mm(o[:, width:2 * width], pT[:, P:2 * P], v[:, 0, col:col + width], start=True, stop=False)
                mm(o[:, width:2 * width], pT[:, 2 * P:3 * P], v[:, 1, col:col + width],
                   start=False, stop=True).then_inc(heads_psum, 1)

            for c in range(10, C_O):
                for i in range(CK):
                    u = c * CK + i
                    if c == 10 and i == 6:
                        transpose_roped(9)
                    if C_INDEX <= c < C_INDEX + 4 and i % 2 == 0:
                        index_scores(4 * (c - C_INDEX) + i // 2)
                    if U_A <= u < U_B:
                        h, step = divmod(u - U_A, 4)
                        if step == 0:
                            if h < 2:
                                pe.wait_ge(idx_relu, IDX_HEADS)
                                pe.wait_ge(qkT_ready, 10)
                            else:
                                pe.wait_ge(og_ready, h - 1)
                            qk_scores(QA + h, KA + h, S0 + h % 2)
                        if step == 2:
                            pe.wait_ge(probs_ready, h + 1)
                            transpose_probs(probs[h % 2], h)
                        if step == 3:
                            pe.wait_ge(probsT_ready, h + 1)
                            weighted_values(probsT[h % 2], S0 + h % 2, h * HD, HD)
                    if U_B <= u < U_OGT:
                        h, step = divmod(u - U_B, 8)
                        if step == 0:
                            pe.wait_ge(og_ready, A_HEADS + h)
                            for n in range(2):
                                qk_scores(QB + 2 * h + n, KB + 2 * h + n, S0 + n)
                        if step == 4:
                            pe.wait_ge(mixed, h + 1)
                            transpose_probs(probs[0], h)
                        if step == 5:
                            pe.wait_ge(probsT_ready, A_HEADS + h + 1)
                            weighted_values(probsT[h % 2], S0, A_W + 2 * h * HD, 2 * HD)
                    if u >= U_OGT and i % 2 == 0:
                        n = (u - U_OGT) // 2
                        pe.wait_ge(og_ready, A_HEADS + B_HEADS)
                        if n >= 2:
                            pe.wait_ge(split_lo, 8 + n - 1)
                        transpose_step(lambda b, r: g[:, r, (2 * n + b) * P:(2 * n + b + 1) * P], T0 + n % 2)
                    w_in_unit(c, i, c % 2)

            def merged_step(t):
                if t % 2 == 0:
                    pe.wait_ge(merged, t // 2 + 1)
                pe.wait_ge(split_lo, 16 + t - 1)
                transpose_step(lambda b, r: stage[:, r, (2 * (t % 2) + b) * P:(2 * (t % 2) + b + 1) * P],
                               T0 + t % 2)

            for n in range(4):
                for branch in range(2):
                    for i in range(4):
                        u = U_O + 8 * n + 4 * branch + i
                        if n > 0 and branch == 0 and i >= 2:
                            merged_step(2 * (n - 1) + i - 2)
                        if i == 0:
                            if n == 0:
                                pe.wait_ge(chunk_out, C_O - 1 + branch)
                            else:
                                pe.wait_ge(tail_out, 2 * n - 1 + branch)
                        if n == 0 and i == 0:
                            pe.wait_ge(split_lo, 8 + 4 * (branch + 1))
                        unit(u, i, 8 * branch + 2 * i, ogT_hi, ogT_lo, 2 * branch, i == 0, i == 3)
            for n in range(4):
                for i in range(CK):
                    if n == 0 and i in (2, 3):
                        merged_step(6 + i - 2)
                    if i == 0:
                        pe.wait_ge(tail_out, 6 + n + 1)
                    if n == 0 and i in (0, 6, 7):
                        pe.wait_ge(split_lo, {0: 22, 6: 23, 7: 24}[i])
                    unit(U_W + CK * n + i, i % RING, 2 * i, hT_hi, hT_lo, 2 * (n % 2), i == 0, i == CK - 1,
                         rows_done=last_rows if n == 3 and i == CK - 1 else None)

        @block.scalar
        def _(act):
            activation = nc.scalar.activation
            act.dma_start(gain_rows[:, :], norm_gain[0].rearrange("(k p) -> k p", p=P)).then_inc(gain_landed, 16)

            def split_hi_step(t, dst, k0, bank):
                act.wait_ge(split_T, t + 1)
                activation(dst[:, bass.ds(k0, 2), :], ps[:, bank, :].rearrange("p (k s) -> p k s", k=2),
                           ACT.Copy).then_inc(split_hi, 1)

            act.wait_ge(gainT_psum, 1)
            activation(gainT[:, :], ps[:, 0, 0:KT], ACT.Copy).then_inc(gainT_ready, 1)
            act.wait_ge(gainT_ready, 1)
            def x_hi(t):
                act.wait_ge(split_T, t + 1)
                for b in range(2):
                    k = 2 * t + b
                    ins = activation(hT_hi[:, k, :], ps[:, 4 + t % 4, b * S:(b + 1) * S], ACT.Copy,
                                     scale=gainT[:, k:k + 1])
                ins.then_inc(split_hi, 1)

            def make_hi(u, slot, turn):
                act.wait_ge(raw_landed[slot], turn * 16 + 16)
                if not isinstance(u, int) or u >= RING:
                    act.wait_ge(unit_done, u - (RING - 1))
                activation(hi[:, slot], raw[:, slot], ACT.Copy).then_inc(hi_ready, 1)

            def make_hi_ahead(c, i):
                make_hi(c * CK + (i + RING), i % RING, c * 2 + (i // RING + 1))

            def chunk_to(c, dst, func=ACT.Copy):
                parity = c[1] if isinstance(c, tuple) else c % 2
                c = c[0] if isinstance(c, tuple) else c
                act.wait_ge(unit_done, c * CK + CK)
                for r in range(RT):
                    ins = activation(dst(r), ps[:, 2 * parity + r, :], func, scale=rstd[:, r:r + 1])
                ins.then_inc(chunk_out, 1)

            def qk_chunk(n, parity, norm, first=False):
                if not first:
                    act.wait_ge(rope_done, n)
                chunk_to((n, parity), lambda r: stage[:, r, :])
                if norm:
                    act.wait_ge(chunk_out, n + 1)
                    for r in range(RT):
                        for h in range(4):
                            at = slice(h * HD, (h + 1) * HD)
                            j = 4 * r + h
                            ins = activation(swapped[:, r, at], stage[:, r, at], ACT.Square,
                                             accum_out=ss_h[:, j:j + 1])
                    ins.then_inc(h_squares, 1)

            def qkT_out(n):
                act.wait_ge(qk_transposed, n + 1)
                activation(qkT[:, bass.ds(n * 4, 4), :],
                           ps[:, T0:T0 + 2, :].rearrange("p a (b s) -> p (a b) s", b=2),
                           ACT.Copy).then_inc(qkT_ready, 1)

            for u in range(CK):
                x_hi(u)
                make_hi(u, u % RING, u // RING)
            for i in range(4, CK):
                if i < 6:
                    r = i - 4
                    junk = qkT[:, 8 * r:8 * r + 8, :].rearrange("p a b -> p (a b)")
                    ins = activation(junk, xr[:, r, :], ACT.Square, accum_out=ss_x[:, r:r + 1])
                    if r == RT - 1:
                        ins.then_inc(x_squares, 1)
                if i == 6:
                    act.wait_ge(reduced, 1)
                    activation(sin_t, red4, ACT.Sin).then_inc(sin_ready, 1)
                    activation(cos_t, absr, ACT.Sin, scale=-1.0, bias=HALF_PI).then_inc(sin_ready, 1)
                make_hi_ahead(0, i)
            for i in range(CK):
                if i == 0:
                    act.wait_ge(rstd_ready, 1)
                    qk_chunk(0, 0, norm=False, first=True)
                if i == 7:
                    act.wait_ge(kiwi_landed, 32)
                    activation(kiwi_hi[:, :, :], kiwi_raw, ACT.Copy).then_inc(kiwi_hi_ready, 1)
                if i == 7:
                    qkT_out(0)
                make_hi_ahead(1, i)
            for c in (2, 3):
                for i in range(CK):
                    if i == 0:
                        qk_chunk(c - 1, (c - 1) % 2, norm=c == 3)
                    if c == 2 and i == 3:
                        act.wait_ge(kiwi_done, 1)
                        for r in range(RT):
                            ins = activation(kst[:, r, :], ps[:, S0 + r, 0:KIWI], ACT.Copy, scale=rstd[:, r:r + 1])
                        ins.then_inc(kiwi_out, 1)
                    if c == 3 and i == 1:
                        act.wait_ge(ki_transposed, 1)
                        activation(kiT[:, :], ps[:, S0, 0:S], ACT.Copy).then_inc(kiT_ready, 1)
                    if i == 7:
                        qkT_out(c - 1)
                    make_hi_ahead(c, i)
            with act.Fori(0, 3) as pair:
                for parity in range(2):
                    c = pair * 2 + (4 + parity)
                    for i in range(CK):
                        if i == 0:
                            qk_chunk(c - 1, 1 - parity, norm=True)
                        if i == 7:
                            qkT_out(c - 1)
                        make_hi_ahead(c, i)

            def exps(tile, buf, n):
                act.wait_ge(neg_max_ready, tile + 1)
                for t, at in enumerate((slice(0, P), slice(P, QB_COLS))):
                    j = 2 * n + t
                    ins = activation(probs[buf][:, at], masked[buf][:, at], ACT.Exp, scale=SCALE,
                                     bias=neg_max[:, j:j + 1], accum_out=sum_p[:, j:j + 1])
                ins.then_inc(probs_ready, 1)

            def probsT_out(head, buf):
                act.wait_ge(probsT_psum, head + 1)
                activation(probsT[buf], ps[:, T0 + buf, 0:QB_COLS], ACT.Copy).then_inc(probsT_ready, 1)

            for c in range(10, C_O):
                for i in range(CK):
                    u = c * CK + i
                    if i == 0:
                        if c == 10:
                            qk_chunk(9, 1, norm=True)
                        elif c <= C_G:
                            at = (c - 1 - C_V) * CW
                            chunk_to(c - 1, lambda r: v[:, r, at:at + CW])
                        elif c <= C_M:
                            at = (c - 1 - C_G) * CW
                            chunk_to(c - 1, lambda r: g[:, r, at:at + CW], ACT.Silu)
                        else:
                            at = (c - 1 - C_M) * CW
                            chunk_to(c - 1, lambda r: m[:, r, at:at + CW],
                                     ACT.Sigmoid if c == C_O - 1 else ACT.Copy)
                    if c == 10 and i == 7:
                        qkT_out(9)
                    if C_INDEX <= c < C_INDEX + 4 and i % 2 == 0:
                        h = 4 * (c - C_INDEX) + i // 2
                        act.wait_ge(idx_scores, h + 1)
                        if h >= 2:
                            act.wait_ge(idx_added, h - 1)
                        else:
                            act.wait_ge(rope_done, 10)
                        activation(rel[h % 2], ps[:, S0 + h % 2, 0:QB_COLS], ACT.Relu).then_inc(idx_relu, 1)
                    if U_A <= u < U_B:
                        h, step = divmod(u - U_A, 4)
                        if step == 0:
                            exps(h, h % 2, h % 2)
                        if step == 2:
                            probsT_out(h, h % 2)
                    if U_B <= u < U_OGT:
                        h, step = divmod(u - U_B, 8)
                        if u == U_B:
                            activation(lam_e, lam_s, ACT.Exp).then_inc(lam_exps, 1)
                        if step == 0:
                            for n in range(2):
                                exps(A_HEADS + 2 * h + n, n, n)
                        if step == 4:
                            probsT_out(A_HEADS + h, h % 2)
                        if step == 5:
                            act.wait_ge(heads_psum, A_HEADS + h + 1)
                            for t in range(RT):
                                ins = activation(masked[t][:, 0:2 * HD], ps[:, S0, t * 2 * HD:(t + 1) * 2 * HD],
                                                 ACT.Square, scale=inv_p[:, t:t + 1], accum_out=ss_o[:, t:t + 1])
                            ins.then_inc(o_squares, 1)
                    if u >= U_OGT and i % 2 == 0:
                        n = (u - U_OGT) // 2
                        split_hi_step(8 + n, ogT_hi, 2 * n, T0 + n % 2)
                        if n >= 1 and n <= 6:
                            act.wait_ge(chunk_out, C_M + n)
                            part = m[:, :, (n - 1) * CW:n * CW]
                            activation(part, part, ACT.Sigmoid).then_inc(gates_ready, 1)
                    make_hi_ahead(c, i)

            def merged_hi(t):
                split_hi_step(16 + t, hT_hi, 2 * t, T0 + t % 2)

            for u in range(U_O, U_END):
                if u == U_O:
                    chunk_to(C_O - 1, lambda r: m[:, r, 7 * CW:8 * CW], ACT.Sigmoid)
                n, step = divmod(u - U_O, 8)
                if 1 <= n <= 4 and step in (2, 3):
                    merged_hi(2 * (n - 1) + step - 2)
                if u + RING < U_END:
                    make_hi(u + RING, u % RING, u // RING + 1)

        @block.vector
        def _(dve):
            tt, stt, ts = nc.vector.tensor_tensor, nc.vector.scalar_tensor_tensor, nc.vector.tensor_scalar
            wrote = [0]

            def mark(ins):
                ins.then_inc(dve_wrote, 1)
                wrote[0] = wrote[0] + 1

            def settle():
                dve.wait_ge(dve_wrote, wrote[0])

            def split_lo_step(t, dst, src_hi, k0, bank):
                dve.wait_ge(split_hi, t + 1)
                tt(dst[:, bass.ds(k0, 2), :], ps[:, bank, :].rearrange("p (k s) -> p k s", k=2),
                   src_hi[:, bass.ds(k0, 2), :].bitcast(F32), ALU.subtract).then_inc(split_lo, 1)

            def reduce_phases():
                dve.wait_ge(consts_landed, 11 * 16)
                mark(nc.vector.tensor_copy(pos_f[:, :], pos_i[:, :]))
                mark(tt(lam_prod[:, 0], lams[:, 0], lams[:, 1], ALU.mult))
                mark(tt(lam_prod[:, 1], lams[:, 2], lams[:, 3], ALU.mult))
                settle()
                for r in range(RT):
                    mark(ts(ang[:, r * 64:(r + 1) * 64], freq, pos_f[:, r:r + 1], None, ALU.mult))
                mark(nc.vector.reduce_sum(lam_s, lam_prod, axis=mybir.AxisListType.X))
                settle()
                mark(ts(turns, ang, 1.0 / 6.283185307179586, ROUND, ALU.mult, ALU.add))
                settle()
                mark(ts(red1, turns, ROUND, None, ALU.subtract))
                settle()
                mark(stt(red2, red1, -TWO_PI_1, ang, ALU.mult, ALU.add))
                settle()
                mark(stt(red3, red1, -TWO_PI_2, red2, ALU.mult, ALU.add))
                settle()
                mark(stt(turns, red1, -TWO_PI_3, red3, ALU.mult, ALU.add))
                settle()
                mark(ts(red4, turns, PI_BELOW, -PI_BELOW, ALU.min, ALU.max))
                settle()
                stt(absr, red4, -1.0, red4, ALU.mult, ALU.max).then_inc(reduced, 1)
            def make_tables():
                dve.wait_ge(sin_ready, 2)
                mark(ts(nsin_t, sin_t, -1.0, None, ALU.mult))
                settle()
                half_shape = [P, 4, HD // 2]
                for r in range(RT):
                    c_r, s_r, ns_r = (t[:, r * 64:(r + 1) * 64] for t in (cos_t, sin_t, nsin_t))
                    for b in range(2):
                        half_b, other = slice(b * 64, b * 64 + 64), slice(64 - b * 64, 128 - b * 64)
                        mark(tt(tab_c[:, :, r, half_b], gains[:, :, half_b],
                                c_r.unsqueeze(1).to_broadcast(half_shape), ALU.mult))
                        mark(tt(tab_s[:, :, r, half_b], gains[:, :, other],
                                (ns_r if b == 0 else s_r).unsqueeze(1).to_broadcast(half_shape), ALU.mult))
                        mark(nc.vector.tensor_copy(tab_ci[:, r, b * 32:b * 32 + 32], c_r[:, 0:64:2]))
                        mark(nc.vector.tensor_copy(tab_si[:, r, b * 32:b * 32 + 32],
                                                   (ns_r if b == 0 else s_r)[:, 0:64:2]))
                mark(ts(sub_gain[:, :], sub_gain[:, :], 1.0 - LAMBDA_INIT, None, ALU.mult))

            def x_lo(t):
                dve.wait_ge(split_hi, t + 1)
                for b in range(2):
                    k = 2 * t + b
                    ins = stt(hT_lo[:, k, :], ps[:, 4 + t % 4, b * S:(b + 1) * S], gainT[:, k:k + 1],
                              hT_hi[:, k, :].bitcast(F32), ALU.mult, ALU.subtract)
                ins.then_inc(split_lo, 1)

            def make_lo(u, slot):
                dve.wait_ge(hi_ready, u + 1)
                tt(lo[:, slot], raw[:, slot], hi[:, slot].bitcast(F32), ALU.subtract).then_inc(lo_ready, 1)

            def make_lo_ahead(c, i):
                make_lo(c * CK + (i + RING), i % RING)

            def heads_view(t, r, hh, dd):
                return t[:, r, :].rearrange("p (h d) -> p h d", d=dd)

            def rope(n, width, cos_of, sin_of, step):
                heads, hw = CW // width, width // 2
                views = [t[:, :, :].rearrange("p r (h d) -> p r h d", d=width) for t in (stage, roped, swapped)]
                src, cos_out, sin_out = views
                if step == 0:
                    if not isinstance(n, int) or n > 0:
                        dve.wait_ge(qk_transposed, n)
                    for r in range(RT):
                        c_tab = cos_of(r).unsqueeze(1).to_broadcast([P, heads, width])
                        mark(tt(cos_out[:, r], src[:, r], c_tab, ALU.mult))
                        for b in range(2):
                            half_b, other = slice(b * hw, (b + 1) * hw), slice((1 - b) * hw, (2 - b) * hw)
                            s_tab = sin_of(r)[:, half_b].unsqueeze(1).to_broadcast([P, heads, hw])
                            mark(tt(sin_out[:, r, :, half_b], src[:, r, :, other], s_tab, ALU.mult))
                else:
                    settle()
                    tt(roped[:, :, :], roped[:, :, :], swapped[:, :, :], ALU.add).then_inc(rope_done, 1)

            def norm_rope(n, i_tab, step):
                if step == 0:
                    dve.wait_ge(r_h_ready, n - 1)
                    src = stage[:, :, :].rearrange("p r (h d) -> p (r h) d", d=HD)
                    mark(tt(src, src, r_h.unsqueeze(2).to_broadcast([P, 8, HD]), ALU.mult))
                elif step == 1:
                    settle()
                    rope(n, HD, lambda r: tab_c[:, bass.ds(i_tab, 1), r, :].squeeze(1),
                         lambda r: tab_s[:, bass.ds(i_tab, 1), r, :].squeeze(1), 0)
                else:
                    rope(n, HD, None, None, 1)

            def index_rope(n, step):
                if step == 0:
                    dve.wait_ge(chunk_out, n + 1)
                    settle()
                if step < 2:
                    rope(n, IDX_DIM, lambda r: tab_ci[:, r, :], lambda r: tab_si[:, r, :], step)

            for u in range(CK):
                x_lo(u)
                make_lo(u, u % RING)
            for i in range(4, CK):
                if i == 5:
                    reduce_phases()
                if i == 7:
                    make_tables()
                make_lo_ahead(0, i)
            for i in range(CK):
                if i == 7:
                    dve.wait_ge(kiwi_hi_ready, 1)
                    tt(kiwi_lo[:, :, :], kiwi_raw, kiwi_hi[:, :, :].bitcast(F32), ALU.subtract).then_inc(kiwi_lo_ready, 1)
                if 1 <= i <= 2:
                    index_rope(0, i - 1)
                make_lo_ahead(1, i)
            for c in (2, 3):
                for i in range(CK):
                    if 1 <= i <= 3:
                        if c == 2:
                            index_rope(1, i - 1)
                        else:
                            norm_rope(2, 0, i - 1)
                    if c == 2 and i == 5:
                        dve.wait_ge(kiwi_out, 1)
                        mark(tt(k_cos, kst[:, :, 0:IDX_DIM], tab_ci, ALU.mult))
                        for b in range(2):
                            half_b, other = slice(b * 32, b * 32 + 32), slice(32 - b * 32, 64 - b * 32)
                            mark(tt(k_swap[:, :, half_b], kst[:, :, other], tab_si[:, :, half_b], ALU.mult))
                        mark(ts(w_idx[:, :, :], kst[:, :, IDX_DIM:KIWI], IDX_SCALE, None, ALU.mult))
                        settle()
                        for b in range(2):
                            ins = tt(kr[:, :, b * IDX_DIM:(b + 1) * IDX_DIM], k_cos, k_swap, ALU.add)
                        ins.then_inc(ki_roped, 1)
                    make_lo_ahead(c, i)
            before = wrote[0]
            for_each = 2 * (1 + 6)
            with dve.Fori(0, 3) as pair:
                wrote[0] = pair * for_each + before
                for parity in range(2):
                    c = pair * 2 + (4 + parity)
                    for i in range(CK):
                        if 1 <= i <= 3:
                            norm_rope(c - 1, pair + parity, i - 1)
                        make_lo_ahead(c, i)
            wrote[0] = before + 3 * for_each

            def masked_max(buf, bank, bias, n, tile):
                dve.wait_ge(scores, tile + 1)
                for t, at in enumerate((slice(0, P), slice(P, QB_COLS))):
                    j = 2 * n + t
                    mark(nc.vector.tensor_tensor_reduce(
                        out=masked[buf][:, at], in0=ps[:, bank, at], in1=bias[:, at], scale=1.0, scalar=MARK,
                        op0=ALU.add, op1=ALU.max, accum_out=max_s[:, j:j + 1]))
                settle()
                ts(neg_max[:, 2 * n:2 * n + 2], max_s[:, 2 * n:2 * n + 2], -SCALE, None,
                   ALU.mult).then_inc(neg_max_ready, 1)

            def topk_round():
                tiles = (slice(0, P), slice(P, QB_COLS))
                settle()
                for t, at in enumerate(tiles):
                    mark(nc.vector.max(top8[:, t], score[:, at]))
                settle()
                for t, at in enumerate(tiles):
                    mark(nc.vector.match_replace(score[:, at], top8[:, t], score[:, at], MARK))

            for c in range(10, C_O):
                for i in range(CK):
                    u = c * CK + i
                    if c == 10 and 1 <= i <= 3:
                        norm_rope(9, 3, i - 1)
                    if C_INDEX <= c < C_INDEX + 4 and i % 2 == 0:
                        h = 4 * (c - C_INDEX) + i // 2
                        if h == 0:
                            dve.wait_ge(causal_ready, 1)
                        dve.wait_ge(idx_relu, h + 1)
                        settle()
                        for t, at in enumerate((slice(0, P), slice(P, QB_COLS))):
                            ins = stt(score[:, at], rel[h % 2][:, at], w_idx[:, t, h:h + 1],
                                      (bias_b if h == 0 else score)[:, at], ALU.mult, ALU.add)
                            if t == 0:
                                mark(ins)
                        ins.then_inc(idx_added, 1)
                        dve.wait_ge(idx_added, h + 1)
                    if c == U_TOPK // CK:
                        topk_round()
                    if u == U_A - 1:
                        settle()
                        mark(ts(bias_a[:, :], score[:, :], 0.5 * MARK, NEG, ALU.is_gt, ALU.mult))
                        settle()
                        mark(tt(bias_a[:, :], bias_a[:, :], bias_b[:, :], ALU.add))
                        settle()
                    if U_A <= u < U_B:
                        h, step = divmod(u - U_A, 4)
                        n = h % 2
                        if step == 0:
                            masked_max(n, S0 + n, bias_a, n, h)
                        if step == 3:
                            dve.wait_ge(probs_ready, h + 1)
                            mark(nc.vector.reciprocal(inv_p[:, 2 * n:2 * n + 2], sum_p[:, 2 * n:2 * n + 2]))
                            dve.wait_ge(heads_psum, h + 1)
                            dve.wait_ge(chunk_out, C_G + 2)
                            settle()
                            for t in range(RT):
                                part = g[:, t, h * HD:(h + 1) * HD]
                                ins = stt(part, ps[:, S0 + n, t * HD:(t + 1) * HD], inv_p[:, 2 * n + t:2 * n + t + 1],
                                          part, ALU.mult, ALU.mult)
                            ins.then_inc(og_ready, 1)
                    if c == C_M and i in (1, 2):
                        r = i - 1
                        if r == 0:
                            dve.wait_ge(chunk_out, C_M)
                        part = g[:, r, A_W:2 * A_W].rearrange("p (h d) -> p h d", d=2 * HD)
                        mark(tt(part, part, sub_gain[:, :].unsqueeze(1).to_broadcast([P, B_HEADS, 2 * HD]), ALU.mult))
                    if U_B <= u < U_OGT:
                        h, step = divmod(u - U_B, 8)
                        if step == 0:
                            for n in range(2):
                                masked_max(n, S0 + n, bias_b, n, A_HEADS + 2 * h + n)
                        if step == 2:
                            dve.wait_ge(probs_ready, A_HEADS + 2 * h + 2)
                            mark(nc.vector.reciprocal(inv_p, sum_p))
                            if h == 0:
                                dve.wait_ge(lam_exps, 1)
                                mark(stt(neg_lam, lam_e[:, 1:2], -LAMBDA_INIT, lam_e[:, 0:1],
                                         ALU.add, ALU.subtract))
                            settle()
                            mark(stt(mix, sum_p[:, 0:2], neg_lam, inv_p[:, 2:4], ALU.mult, ALU.mult))
                            settle()
                            for t, at in enumerate((slice(0, P), slice(P, QB_COLS))):
                                ins = stt(probs[0][:, at], probs[1][:, at], mix[:, t:t + 1], probs[0][:, at],
                                          ALU.mult, ALU.add)
                            ins.then_inc(mixed, 1)
                        if step == 6:
                            dve.wait_ge(r_o_ready, h + 1)
                            mark(tt(f_o, r_o, inv_p[:, 0:2], ALU.mult))
                            settle()
                            for t in range(RT):
                                at = A_W + h * 2 * HD
                                part = g[:, t, at:at + 2 * HD]
                                ins = stt(part, ps[:, S0, t * 2 * HD:(t + 1) * 2 * HD], f_o[:, t:t + 1], part,
                                          ALU.mult, ALU.mult)
                            ins.then_inc(og_ready, 1)
                    if u >= U_OGT and i % 2 == 0:
                        n = (u - U_OGT) // 2
                        split_lo_step(8 + n, ogT_lo, ogT_hi, 2 * n, T0 + n % 2)
                    make_lo_ahead(c, i)

            def add_residual(u, n):
                dve.wait_ge(unit_done, u)
                if n == 0:
                    dve.wait_ge(res_landed, 16)
                part = g[:, :, n * CW:(n + 1) * CW]
                bank = 2 * (n % 2)
                tt(part, ps[:, bank:bank + 2, :], part, ALU.add).then_inc(tail_out, 1)

            for u in range(U_O, U_END):
                n, step = divmod(u - U_O, 8)
                if n < 4 and step == 4:
                    if n == 0:
                        dve.wait_ge(gates_ready, 6)
                        dve.wait_ge(chunk_out, C_O)
                    dve.wait_ge(unit_done, u)
                    part = m[:, :, n * CW:(n + 1) * CW]
                    tt(part, ps[:, 0:2, :], part, ALU.mult).then_inc(tail_out, 1)
                if 1 <= n <= 4 and step == 0:
                    dve.wait_ge(unit_done, u)
                    a_part, b_part = (m[:, :, b * D + (n - 1) * CW:b * D + n * CW] for b in range(2))
                    tt(b_part, ps[:, 2:4, :], b_part, ALU.mult).then_inc(tail_out, 1)
                    dve.wait_ge(tail_out, 2 * n)
                    if n >= 2:
                        dve.wait_ge(split_T, 16 + 2 * (n - 1))
                    tt(stage[:, :, :], a_part, b_part, ALU.add).then_inc(merged, 1)
                if 1 <= n <= 4 and step in (2, 3):
                    t = 2 * (n - 1) + step - 2
                    split_lo_step(16 + t, hT_lo, hT_hi, 2 * t, T0 + t % 2)
                if u >= U_W + CK and step == 0:
                    add_residual(u, n - 5)
                if u + RING < U_END:
                    make_lo(u + RING, u % RING)
            for r in range(RT):
                if r == 0:
                    dve.wait_ge(last_rows, 1)
                else:
                    dve.wait_ge(unit_done, U_END)
                part = g[:, r, 3 * CW:4 * CW]
                tt(part, ps[:, 2 + r, :], part, ALU.add).then_inc(tail_out, 1)


_INS = ["x", "positions", "inv_freq", "norm_gain", "w_in", "a_q_gain", "a_k_gain", "b_q_gain", "b_k_gain",
        "lambda_q1", "lambda_k1", "lambda_q2", "lambda_k2", "b_subln_gain", "w_o_a", "w_o_b", "w_out"]


def kernel(**inputs):
    import numpy as _np
    import concourse.bacc as _bacc
    from concourse import mybir as _mybir
    from concourse.bass_utils import run_bass_kernel_spmd as _run

    exponents = _np.arange(0, HD, 2, dtype=_np.float32) / _np.float32(HD)
    freqs = (_np.float32(10000.0) ** -exponents).astype(_np.float32)[None]

    nc = _bacc.Bacc("TRN2", target_bir_lowering=False, num_devices=1)
    arrays, args = {}, []
    for name in _INS:
        a = freqs if name == "inv_freq" else _np.ascontiguousarray(inputs[name])
        arrays[f"in_{name}"] = a
        args.append(nc.dram_tensor(f"in_{name}", a.shape, _mybir.dt.from_np(a.dtype), kind="ExternalInput").ap())
    args.append(nc.dram_tensor("out_0", (1, S, D), _mybir.dt.from_np(_np.dtype("float32")),
                               kind="ExternalOutput").ap())
    build_layer(nc, *args)
    return _run(nc, [arrays], core_ids=[0]).results[0]["out_0"]
```

```python
from contextlib import ExitStack

import concourse.bass as bass
from concourse import mybir
from concourse.alu_op_type import AluOpType as ALU

ACT = mybir.ActivationFunctionType
F32 = mybir.dt.float32
F32R = mybir.dt.float32r
I32 = mybir.dt.int32

P = 128
D = 2048
S = 256
RT = S // P
KT = D // P
HD = 128
IDX_HEADS, IDX_DIM = 16, 64
TOPK = S // 4
A_HEADS, B_HEADS = 8, 4
NORM_EPS, SUBLN_EPS = 1e-6, 1e-5
LAMBDA_INIT = 0.2
SCALE = HD ** -0.5
IDX_SCALE = IDX_HEADS ** -0.5 * IDX_DIM ** -0.5

CW = 512
X_CUTS = (0, 256, 512, 1024, 1536, 2048)
CK = 8
RING = 4
WARM_A, WARM_B = 6, 2
KIWI = IDX_DIM + IDX_HEADS
IDX_W = (384, 384, 256 + KIWI)
IDX_BLOCKS = tuple(w // P for w in IDX_W)
A_W = A_HEADS * HD

COL = {}
_at = 0
for _name, _width in (("qa", A_W), ("ka", A_W), ("va", A_W), ("ga", A_W), ("qi", A_W), ("kiwi", KIWI),
                      ("qb", A_W), ("kb", A_W), ("vb", A_W), ("gb", A_W), ("ma", D), ("mb", D)):
    COL[_name] = _at
    _at += _width
IN_COLS = _at

C_QK, C_V, C_G, C_M = 3, 11, 15, 19
C_O = 27
U_O = C_O * CK
U_W = U_O + 8 * 4
U_END = U_W + 4 * CK
C_INDEX = C_V + 1
U_TOPK = (C_INDEX + 4) * CK
U_A = U_TOPK + CK
U_B = U_A + 4 * A_HEADS
U_OGT = U_B + 8 * B_HEADS
assert U_OGT + 16 == U_O

NEG = -1.0e30
MARK = -3.0e38
TWO_PI_1 = 6.28125
TWO_PI_2 = 0.0019350051879882812
TWO_PI_3 = 3.0199159819e-07
ROUND = 12582912.0
PI_BELOW = 3.1415925
HALF_PI = 1.5707963267948966


def chunk_width(c):
    return IDX_W[c] if c < C_QK else CW


def chunk_bank(c):
    return 2 * ((c + 1) % 2)


def build_layer(nc, x, positions, inv_freq, norm_gain, w_in, a_q_gain, a_k_gain, b_q_gain, b_k_gain,
                lambda_q1, lambda_k1, lambda_q2, lambda_k2, b_subln_gain, w_o_a, w_o_b, w_out, out):
    x_rows = x[0].rearrange("(r p) d -> p r d", p=P)
    out_rows = out[0].rearrange("(r p) d -> p r d", p=P)

    with ExitStack() as ctx:
        place = [-(-nc.sbuf_base // 64) * 64]

        def sb(name, shape, dt=F32, at=None):
            size = 4
            for n in shape[1:]:
                size *= n
            offset = place[0] if at is None else at
            if at is None:
                place[0] += -(-size // 64) * 64
                assert place[0] <= nc.sbuf_usable_end, (name, place[0])
            return nc.alloc_sbuf_tensor_at(name, shape, dt, offset=offset)

        def sem(name):
            return ctx.enter_context(nc.semaphore(name))

        raw = sb("raw", [P, RING, 2, CW])
        hi = sb("hi", [P, RING, 2, CW], F32R)
        lo = sb("lo", [P, RING, 2, CW], F32R)
        hT_hi = sb("hT_hi", [P, KT, S], F32R)
        hT_lo = sb("hT_lo", [P, KT, S], F32R)
        qk_at = place[0]
        qkT = sb("qkT", [P, 5 * 8, S])
        ogT_hi = sb("ogT_hi", [P, KT, S], F32R, at=qk_at)
        ogT_lo = sb("ogT_lo", [P, KT, S], F32R, at=qk_at + 4 * KT * S)
        QI, QA, KA, QB, KB = 0, 8, 16, 24, 32
        v = sb("v", [P, RT, 2 * A_W])
        g = sb("g", [P, RT, 2 * A_W])
        m = sb("m", [P, RT, 2 * D])
        xr = m[:, 0, :].rearrange("p (r d) -> p r d", r=RT)

        ident = sb("ident", [P, P])
        stage = sb("stage", [P, RT, CW])
        roped = sb("roped", [P, RT, CW])
        swapped = sb("swapped", [P, RT, CW])
        QB_COLS = 3 * P
        work_flat = [stage[:, :, :].rearrange("p r n -> p (r n)"),
                     roped[:, :, :].rearrange("p r n -> p (r n)"),
                     swapped[:, :, :].rearrange("p r n -> p (r n)")]
        masked = [work_flat[0][:, i * QB_COLS:(i + 1) * QB_COLS] for i in range(2)]
        probs = [work_flat[1][:, i * QB_COLS:(i + 1) * QB_COLS] for i in range(2)]
        probsT = [work_flat[2][:, i * QB_COLS:(i + 1) * QB_COLS] for i in range(2)]
        rel = masked
        score = sb("score", [P, QB_COLS])
        bias_a = sb("bias_a", [P, QB_COLS])
        bias_b = sb("bias_b", [P, QB_COLS])
        kiT = sb("kiT", [P, S])
        w_idx = sb("w_idx", [P, RT, IDX_HEADS])
        sub_gain = sb("sub_gain", [P, 2 * HD])
        gain_rows = sb("gain_rows", [KT, P])
        gainT = sb("gainT", [P, KT])
        top8 = sb("top8", [P, 2, 8])
        pos_i = sb("pos_i", [P, RT], I32)
        pos_f = sb("pos_f", [P, RT])
        half = sb("half", [P, 8])
        small = sb("small", [P, 96])
        ss_x, ms_x, rstd = small[:, 0:2], small[:, 2:4], small[:, 4:6]
        ss_h, ms_h, r_h = small[:, 8:16], small[:, 16:24], small[:, 24:32]
        lam_s, lam_e, neg_lam = small[:, 32:34], small[:, 34:36], small[:, 36:37]
        max_s, neg_max, sum_p = small[:, 40:44], small[:, 44:48], small[:, 48:52]
        inv_p, mix = small[:, 52:56], small[:, 56:58]
        ss_o, ms_o, r_o, f_o = small[:, 60:62], small[:, 62:64], small[:, 64:66], small[:, 66:68]

        v0 = v[:, 0, :]
        gains = v0[:, 0:512].rearrange("p (i d) -> p i d", i=4)
        lams = v0[:, 512:1024].rearrange("p (i d) -> p i d", i=4)
        lam_prod = v0[:, 1024:1280].rearrange("p (i d) -> p i d", i=2)
        v1 = v[:, 1, :]
        freq = v1[:, 0:64]

        def phases(n):
            return v1[:, 64 + 128 * n:192 + 128 * n]

        ang, turns, red1, red2, red3, red4, absr, sin_t, cos_t, nsin_t = (phases(n) for n in range(10))
        kst = v1[:, 1408:1568].rearrange("p (r n) -> p r n", r=RT)
        k_cos = v1[:, 1568:1696].rearrange("p (r n) -> p r n", r=RT)
        k_swap = v1[:, 1696:1824].rearrange("p (r n) -> p r n", r=RT)
        kr = v0[:, 1280:1536].rearrange("p (r n) -> p r n", r=RT)
        tab_c = g[:, 0, 0:1024].rearrange("p (i r d) -> p i r d", i=4, r=RT)
        tab_s = g[:, 0, 1024:2048].rearrange("p (i r d) -> p i r d", i=4, r=RT)
        tab_ci = g[:, 1, 0:128].rearrange("p (r d) -> p r d", r=RT)
        tab_si = g[:, 1, 128:256].rearrange("p (r d) -> p r d", r=RT)

        ps = ctx.enter_context(nc.psum_tensor("ps", [P, 8, CW], F32))
        T0, S0 = 4, 6

        x_landed = [sem(f"x_landed_{i}") for i in range(len(X_CUTS) - 1)]
        consts_landed = sem("consts_landed")
        gain_landed = sem("gain_landed")
        raw_landed = [sem(f"raw_landed_{i}") for i in range(RING)]
        res_landed = sem("res_landed")
        out_landed = sem("out_landed")
        ident_ready = sem("ident_ready")
        causal_ready = sem("causal_ready")
        pool_wrote = sem("pool_wrote")
        hi_ready, lo_ready, unit_done = sem("hi_ready"), sem("lo_ready"), sem("unit_done")
        chunk_out, tail_out = sem("chunk_out"), sem("tail_out")
        split_T, split_hi, split_lo = sem("split_T"), sem("split_hi"), sem("split_lo")
        gainT_psum, gainT_ready = sem("gainT_psum"), sem("gainT_ready")
        reduced, sin_ready = sem("reduced"), sem("sin_ready")
        lam_exps = sem("lam_exps")
        x_squares, rstd_ready = sem("x_squares"), sem("rstd_ready")
        h_squares, r_h_ready, rope_done = sem("h_squares"), sem("r_h_ready"), sem("rope_done")
        qk_transposed, qkT_ready = sem("qk_transposed"), sem("qkT_ready")
        idx_scores, idx_relu, idx_added = sem("idx_scores"), sem("idx_relu"), sem("idx_added")
        scores, neg_max_ready, probs_ready = sem("scores"), sem("neg_max_ready"), sem("probs_ready")
        probsT_psum, probsT_ready, heads_psum, og_ready = (sem("probsT_psum"), sem("probsT_ready"),
                                                           sem("heads_psum"), sem("og_ready"))
        mixed = sem("mixed")
        o_squares, r_o_ready = sem("o_squares"), sem("r_o_ready")
        gates_ready = sem("gates_ready")
        merged = sem("merged")
        last_rows = sem("last_rows")
        dve_wrote, act_wrote = sem("dve_wrote"), sem("act_wrote")

        block = ctx.enter_context(nc.Block())

        @block.sync
        def _(sp):
            def load_x(j):
                at = slice(X_CUTS[j], X_CUTS[j + 1])
                sp.dma_start(xr[:, :, at], x_rows[:, :, at]).then_inc(x_landed[j], 16)

            def load(slot, u, weights, k0, col, width=CW):
                if not isinstance(u, int) or u >= RING:
                    sp.wait_ge(lo_ready, u - (RING - 1))
                src = weights[0][k0 * P:(k0 + 2) * P, bass.ds(col, width)].rearrange("(k p) n -> p k n", p=P)
                sp.dma_start(raw[:, slot, :, 0:width], src).then_inc(raw_landed[slot], 16)

            def load_chunk(c, col, width=CW):
                for i in range(CK):
                    load(i % RING, c * CK + i, w_in, 2 * i, col, width)

            for i in range(CK):
                if i <= 3:
                    load_x(i)
                if i == 3:
                    load_x(4)
                if i == 4:
                    sp.dma_start(pos_i[:, :], positions[0].rearrange("(r p) -> p r", p=P),
                                  allow_slow_non_contiguous=True).then_inc(consts_landed, 16)
                    sp.dma_start(freq, inv_freq[0].partition_broadcast(P)).then_inc(consts_landed, 16)
                    for j, row in enumerate((a_q_gain, a_k_gain, b_q_gain, b_k_gain)):
                        sp.dma_start(gains[:, j], row[0].partition_broadcast(P)).then_inc(consts_landed, 16)
                    for j, row in enumerate((lambda_q1, lambda_k1, lambda_q2, lambda_k2)):
                        sp.dma_start(lams[:, j], row[0].partition_broadcast(P)).then_inc(consts_landed, 16)
                    sp.dma_start(sub_gain[:, :], b_subln_gain[0].partition_broadcast(P)).then_inc(consts_landed, 16)
                load(i % RING, i, w_in, 2 * i, COL["qi"], IDX_W[0])
            load_chunk(1, COL["qi"] + IDX_W[0], IDX_W[1])
            load_chunk(2, COL["qi"] + IDX_W[0] + IDX_W[1], IDX_W[2])
            with sp.Fori(0, 2) as branch:
                with sp.Fori(0, 4) as n:
                    load_chunk(C_QK + branch * 4 + n, branch * COL["qb"] + n * CW)
            for c, name in ((C_V, "va"), (C_V + 2, "vb"), (C_G, "ga"), (C_G + 2, "gb")):
                with sp.Fori(0, 2) as n:
                    load_chunk(n + c, n * CW + COL[name])
            with sp.Fori(0, 8) as n:
                load_chunk(n + C_M, n * CW + COL["ma"])
            for n in range(4):
                for b, weights in enumerate((w_o_a, w_o_b)):
                    for i in range(4):
                        load(i, U_O + 8 * n + 4 * b + i, weights, 2 * i, n * CW)
                if n == 0:
                    sp.wait_ge(split_lo, 16)
                    sp.dma_start(g[:, :, :], x_rows).then_inc(res_landed, 16)
            for n in range(4):
                for i in range(CK):
                    load(i % RING, U_W + CK * n + i, w_out, 2 * i, n * CW)
            for n in range(3):
                sp.wait_ge(tail_out, 8 + n + 1)
                sp.dma_start(out_rows[:, :, n * CW:(n + 1) * CW],
                             g[:, :, n * CW:(n + 1) * CW]).then_inc(out_landed, 16)
            for r in range(RT):
                sp.wait_ge(tail_out, 11 + r + 1)
                sp.dma_start(out_rows[:, r, 3 * CW:4 * CW], g[:, r, 3 * CW:4 * CW]).then_inc(out_landed, 16)
            sp.wait_ge(out_landed, 5 * 16)

        @block.gpsimd
        def _(pool):
            nc.gpsimd.memset(ident[:, :], 0.0).then_inc(pool_wrote, 1)
            nc.gpsimd.memset(bias_b[:, :], 0.0).then_inc(pool_wrote, 1)
            nc.gpsimd.memset(half[:, :], -0.5).then_inc(pool_wrote, 1)
            pool.wait_ge(pool_wrote, 3)
            nc.gpsimd.affine_select(out=ident[:, :], in_=ident[:, :], compare_op=ALU.not_equal, fill=1.0,
                                    base=0, pattern=[[-1, P]], channel_multiplier=1).then_inc(ident_ready, 1)
            for start in (0, 2 * P):
                blk = bias_b[:, start:start + P]
                last = nc.gpsimd.affine_select(out=blk, in_=blk, compare_op=ALU.is_ge, fill=NEG, base=0,
                                               pattern=[[-1, P]], channel_multiplier=1)
            last.then_inc(causal_ready, 1)
            wrote = [3]

            def root(out, mean, total, n, width, eps):
                nc.gpsimd.tensor_scalar(mean, total, 1.0 / n, eps, ALU.mult, ALU.add).then_inc(pool_wrote, 1)
                wrote[0] = wrote[0] + 1
                pool.wait_ge(pool_wrote, wrote[0])
                return nc.gpsimd.tensor_tensor(out, mean, half[:, 0:width], ALU.pow)

            pool.wait_ge(x_squares, 1)
            root(rstd, ms_x, ss_x, D, RT, NORM_EPS).then_inc(rstd_ready, 1)
            for n in range(8):
                pool.wait_ge(h_squares, n + 1)
                root(r_h, ms_h, ss_h, HD, 8, NORM_EPS).then_inc(r_h_ready, 1)
            for h in range(B_HEADS):
                pool.wait_ge(o_squares, h + 1)
                root(r_o, ms_o, ss_o, 2 * HD, RT, SUBLN_EPS).then_inc(r_o_ready, 1)

        @block.tensor
        def _(pe):
            mm = nc.tensor.matmul

            def unit(u, slot, k0, s_hi, s_lo, bank, first, last, width=CW, rows_done=None):
                w_hi, w_lo = (t[:, slot, :, 0:width] for t in (hi, lo))
                pe.wait_ge(lo_ready, u + 1)
                order = [(j, r) for j in range(2) for r in range(RT)]
                if rows_done is not None:
                    order.sort(key=lambda jr: jr[1])
                for j, r in order:
                    a_hi = s_hi[:, k0 + j, r * P:(r + 1) * P]
                    a_lo = s_lo[:, k0 + j, r * P:(r + 1) * P]
                    o = ps[:, bank + r, 0:width]
                    mm(o, a_hi, w_hi[:, j], start=first and j == 0, stop=False)
                    mm(o, a_hi, w_lo[:, j], start=False, stop=False)
                    ins = mm(o, a_lo, w_hi[:, j], start=False, stop=last and j == 1)
                    if rows_done is not None and j == 1 and r == 0:
                        ins.then_inc(rows_done, 1)
                ins.then_inc(unit_done, 1)

            def first_unit():
                tiles = [(j, r) for j in range(2) for r in range(RT)]
                for parts, operand, part in ((hi_ready, hT_hi, hi), (hi_ready, hT_lo, hi), (lo_ready, hT_hi, lo)):
                    pe.wait_ge(parts, 1)
                    for j, r in tiles:
                        ins = mm(ps[:, chunk_bank(0) + r, 0:IDX_W[0]], operand[:, j, r * P:(r + 1) * P],
                                 part[:, 0, j, 0:IDX_W[0]], start=part is hi and operand is hT_hi and j == 0,
                                 stop=False)
                ins.then_inc(unit_done, 1)

            def w_in_unit(c, i, bank, width=CW):
                if isinstance(c, int) and c == 0:
                    pe.wait_ge(split_lo, i + 1)
                    if i == 0:
                        first_unit()
                        return
                if i == 0 and (not isinstance(c, int) or c >= 2):
                    pe.wait_ge(chunk_out, c - 1)
                unit(c * CK + i, i % RING, 2 * i, hT_hi, hT_lo, bank, i == 0, i == CK - 1, width)

            def transpose_roped(n, blocks=4):
                pe.wait_ge(rope_done, n + 1)
                if not isinstance(n, int) or n > 0:
                    pe.wait_ge(qkT_ready, n)
                for b in range(blocks):
                    for r in range(RT):
                        o = ps[:, T0 + b // 2, (b % 2) * S + r * P:(b % 2) * S + (r + 1) * P]
                        ins = nc.tensor.transpose(o, roped[:, r, b * P:(b + 1) * P], ident[:, :])
                if isinstance(n, int) and n == C_QK - 1:
                    for r in range(RT):
                        ins = nc.tensor.transpose(ps[:, T0 + 1, r * P:(r + 1) * P], kr[:, r, :], ident[:, :])
                ins.then_inc(qk_transposed, 1)

            def transpose_step(rows, bank):
                for b in range(2):
                    for r in range(RT):
                        o = ps[:, bank, b * S + r * P:b * S + (r + 1) * P]
                        ins = nc.tensor.transpose(o, rows(b, r), ident[:, :])
                ins.then_inc(split_T, 1)

            def warm_up(count):
                for _ in range(count):
                    mm(ps[:, S0 + 1, 0:P], ident[:, :], ident[:, :], start=True, stop=True)

            pe.wait_ge(ident_ready, 1)
            warm_up(WARM_A)
            pe.wait_ge(gain_landed, 16)
            nc.tensor.transpose(ps[:, 0, 0:KT], gain_rows[:, :], ident[0:KT, 0:KT]).then_inc(gainT_psum, 1)

            def transpose_x(n):
                if 256 * n in X_CUTS:
                    pe.wait_ge(x_landed[X_CUTS.index(256 * n)], 16)
                if n >= 4:
                    pe.wait_ge(split_lo, n - 3)
                transpose_step(lambda b, r: xr[:, r, (2 * n + b) * P:(2 * n + b + 1) * P], 4 + n % 4)

            transpose_x(0)
            transpose_x(1)
            warm_up(WARM_B)
            for c in range(C_QK + 2):
                for i in range(CK):
                    if c == 0 and i in (1, 2, 3):
                        transpose_x(2 * i)
                        transpose_x(2 * i + 1)
                    if c == 1 and i == 0:
                        pe.wait_ge(gainT_ready, 1)
                    if c == 1 and i == 6:
                        pe.wait_ge(split_lo, 8)
                    if c >= 1 and i == 6:
                        transpose_roped(c - 1, IDX_BLOCKS[c - 1] if c <= C_QK else 4)
                    w_in_unit(c, i, chunk_bank(c), chunk_width(c))
            with pe.Fori(0, 3) as pair:
                for turn in range(2):
                    c = pair * 2 + (C_QK + 2 + turn)
                    for i in range(CK):
                        if i == 6:
                            transpose_roped(c - 1)
                        w_in_unit(c, i, chunk_bank(C_QK + 2 + turn))

            def index_scores(h):
                if h < 2:
                    pe.wait_ge(qkT_ready, C_QK)
                else:
                    pe.wait_ge(idx_relu, h - 1)
                a = (h % 2) * IDX_DIM
                q = qkT[a:a + IDX_DIM, QI + h // 2, :]
                k = kiT[a:a + IDX_DIM, :]
                o = ps[:, S0 + h % 2, :]
                mm(o[:, 0:P], q[:, 0:P], k[:, 0:P], start=True, stop=True)
                mm(o[:, P:P + S], q[:, P:S], k[:, :], start=True, stop=True).then_inc(idx_scores, 1)

            def qk_scores(q_block, k_block, bank):
                o = ps[:, bank, :]
                mm(o[:, 0:P], qkT[:, q_block, 0:P], qkT[:, k_block, 0:P], start=True, stop=True)
                mm(o[:, P:P + S], qkT[:, q_block, P:S], qkT[:, k_block, :],
                   start=True, stop=True).then_inc(scores, 1)

            def transpose_probs(src, head):
                for b in range(3):
                    ins = nc.tensor.transpose(ps[:, T0 + head % 2, b * P:(b + 1) * P],
                                              src[:, b * P:(b + 1) * P], ident[:, :])
                ins.then_inc(probsT_psum, 1)

            def weighted_values(pT, bank, col, width):
                o = ps[:, bank, :]
                mm(o[:, 0:width], pT[:, 0:P], v[:, 0, col:col + width], start=True, stop=True)
                mm(o[:, width:2 * width], pT[:, P:2 * P], v[:, 0, col:col + width], start=True, stop=False)
                mm(o[:, width:2 * width], pT[:, 2 * P:3 * P], v[:, 1, col:col + width],
                   start=False, stop=True).then_inc(heads_psum, 1)

            for c in range(C_V, C_O):
                for i in range(CK):
                    u = c * CK + i
                    if c == C_V and i == 6:
                        transpose_roped(C_V - 1)
                    if C_INDEX <= c < C_INDEX + 4 and i % 2 == 0:
                        index_scores(4 * (c - C_INDEX) + i // 2)
                    if U_A <= u < U_B:
                        h, step = divmod(u - U_A, 4)
                        if step == 0:
                            if h < 2:
                                pe.wait_ge(idx_relu, IDX_HEADS)
                                pe.wait_ge(qkT_ready, C_V)
                            else:
                                pe.wait_ge(og_ready, h - 1)
                            qk_scores(QA + h, KA + h, S0 + h % 2)
                        if step == 2:
                            pe.wait_ge(probs_ready, h + 1)
                            transpose_probs(probs[h % 2], h)
                        if step == 3:
                            pe.wait_ge(probsT_ready, h + 1)
                            weighted_values(probsT[h % 2], S0 + h % 2, h * HD, HD)
                    if U_B <= u < U_OGT:
                        h, step = divmod(u - U_B, 8)
                        if step == 0:
                            pe.wait_ge(og_ready, A_HEADS + h)
                            for n in range(2):
                                qk_scores(QB + 2 * h + n, KB + 2 * h + n, S0 + n)
                        if step == 4:
                            pe.wait_ge(mixed, h + 1)
                            transpose_probs(probs[0], h)
                        if step == 5:
                            pe.wait_ge(probsT_ready, A_HEADS + h + 1)
                            weighted_values(probsT[h % 2], S0, A_W + 2 * h * HD, 2 * HD)
                    if u >= U_OGT and i % 2 == 0:
                        n = (u - U_OGT) // 2
                        pe.wait_ge(og_ready, A_HEADS + B_HEADS)
                        if n >= 2:
                            pe.wait_ge(split_lo, 8 + n - 1)
                        transpose_step(lambda b, r: g[:, r, (2 * n + b) * P:(2 * n + b + 1) * P], T0 + n % 2)
                    w_in_unit(c, i, chunk_bank(c))

            def merged_step(t):
                if t % 2 == 0:
                    pe.wait_ge(merged, t // 2 + 1)
                pe.wait_ge(split_lo, 16 + t - 1)
                transpose_step(lambda b, r: stage[:, r, (2 * (t % 2) + b) * P:(2 * (t % 2) + b + 1) * P],
                               T0 + t % 2)

            for n in range(4):
                for branch in range(2):
                    for i in range(4):
                        u = U_O + 8 * n + 4 * branch + i
                        if n > 0 and branch == 0 and i >= 2:
                            merged_step(2 * (n - 1) + i - 2)
                        if i == 0:
                            if n == 0:
                                pe.wait_ge(chunk_out, C_O - 1 + branch)
                            else:
                                pe.wait_ge(tail_out, 2 * n - 1 + branch)
                        if n == 0 and i == 0:
                            pe.wait_ge(split_lo, 8 + 4 * (branch + 1))
                        unit(u, i, 8 * branch + 2 * i, ogT_hi, ogT_lo, 2 * branch, i == 0, i == 3)
            for n in range(4):
                for i in range(CK):
                    if n == 0 and i in (2, 3):
                        merged_step(6 + i - 2)
                    if i == 0:
                        pe.wait_ge(tail_out, 6 + n + 1)
                    if n == 0 and i in (0, 6, 7):
                        pe.wait_ge(split_lo, {0: 22, 6: 23, 7: 24}[i])
                    unit(U_W + CK * n + i, i % RING, 2 * i, hT_hi, hT_lo, 2 * (n % 2), i == 0, i == CK - 1,
                         rows_done=last_rows if n == 3 and i == CK - 1 else None)

        @block.scalar
        def _(act):
            activation = nc.scalar.activation
            act.dma_start(gain_rows[:, :], norm_gain[0].rearrange("(k p) -> k p", p=P)).then_inc(gain_landed, 16)

            def split_hi_step(t, dst, k0, bank):
                act.wait_ge(split_T, t + 1)
                activation(dst[:, bass.ds(k0, 2), :], ps[:, bank, :].rearrange("p (k s) -> p k s", k=2),
                           ACT.Copy).then_inc(split_hi, 1)

            act.wait_ge(gainT_psum, 1)
            activation(gainT[:, :], ps[:, 0, 0:KT], ACT.Copy).then_inc(gainT_ready, 1)
            act.wait_ge(gainT_ready, 1)
            def x_hi(t):
                act.wait_ge(split_T, t + 1)
                for b in range(2):
                    k = 2 * t + b
                    ins = activation(hT_hi[:, k, :], ps[:, 4 + t % 4, b * S:(b + 1) * S], ACT.Copy,
                                     scale=gainT[:, k:k + 1])
                ins.then_inc(split_hi, 1)

            def make_hi(u, slot, turn, width=CW):
                act.wait_ge(raw_landed[slot], turn * 16 + 16)
                if not isinstance(u, int) or u >= RING:
                    act.wait_ge(unit_done, u - (RING - 1))
                activation(hi[:, slot, :, 0:width], raw[:, slot, :, 0:width], ACT.Copy).then_inc(hi_ready, 1)

            def make_hi_ahead(c, i):
                width = chunk_width(c + (i + RING) // CK) if isinstance(c, int) else CW
                make_hi(c * CK + (i + RING), i % RING, c * 2 + (i // RING + 1), width)

            def chunk_to(c, dst, func=ACT.Copy, bank=None, width=CW):
                bank = chunk_bank(c) if bank is None else bank
                act.wait_ge(unit_done, c * CK + CK)
                for r in range(RT):
                    ins = activation(dst(r), ps[:, bank + r, 0:width], func, scale=rstd[:, r:r + 1])
                if isinstance(c, int) and c == C_QK - 1:
                    for r in range(RT):
                        ins = activation(kst[:, r, :], ps[:, bank + r, width:width + KIWI], func,
                                         scale=rstd[:, r:r + 1])
                ins.then_inc(chunk_out, 1)

            def index_chunk(n):
                if n > 0:
                    act.wait_ge(rope_done, n)
                width = IDX_BLOCKS[n] * P
                chunk_to(n, lambda r: stage[:, r, 0:width], width=width)

            def qk_chunk(n, bank):
                act.wait_ge(rope_done, n)
                chunk_to(n, lambda r: stage[:, r, :], bank=bank)
                act.wait_ge(chunk_out, n + 1)
                for r in range(RT):
                    for h in range(4):
                        at = slice(h * HD, (h + 1) * HD)
                        j = 4 * r + h
                        ins = activation(swapped[:, r, at], stage[:, r, at], ACT.Square,
                                         accum_out=ss_h[:, j:j + 1])
                ins.then_inc(h_squares, 1)

            def qkT_out(n):
                act.wait_ge(qk_transposed, n + 1)
                activation(qkT[:, bass.ds((n - C_QK) * 4 + QA, 4), :],
                           ps[:, T0:T0 + 2, :].rearrange("p a (b s) -> p (a b) s", b=2),
                           ACT.Copy).then_inc(qkT_ready, 1)

            def index_T_out(n):
                act.wait_ge(qk_transposed, n + 1)
                first, blocks = QI + sum(IDX_BLOCKS[:n]), IDX_BLOCKS[n]
                ins = activation(qkT[:, first:first + blocks, :],
                                 ps[:, T0:T0 + 2, :].rearrange("p a (b s) -> p (a b) s", b=2)[:, 0:blocks],
                                 ACT.Copy)
                if n == C_QK - 1:
                    ins = activation(kiT[:, :], ps[:, T0 + 1, 0:S], ACT.Copy)
                ins.then_inc(qkT_ready, 1)

            for u in range(CK):
                x_hi(u)
                make_hi(u, u % RING, u // RING, IDX_W[0])
            for i in range(4, CK):
                if i < 6:
                    r = i - 4
                    junk = qkT[:, 8 * r:8 * r + 8, :].rearrange("p a b -> p (a b)")
                    ins = activation(junk, xr[:, r, :], ACT.Square, accum_out=ss_x[:, r:r + 1])
                    if r == RT - 1:
                        ins.then_inc(x_squares, 1)
                if i == 6:
                    act.wait_ge(reduced, 1)
                    activation(sin_t, red4, ACT.Sin).then_inc(sin_ready, 1)
                    activation(cos_t, absr, ACT.Sin, scale=-1.0, bias=HALF_PI).then_inc(sin_ready, 1)
                make_hi_ahead(0, i)
            for c in range(1, C_QK + 2):
                for i in range(CK):
                    if i == 0:
                        if c == 1:
                            act.wait_ge(rstd_ready, 1)
                        if c <= C_QK:
                            index_chunk(c - 1)
                        else:
                            qk_chunk(c - 1, chunk_bank(c - 1))
                    if i == 7:
                        (index_T_out if c <= C_QK else qkT_out)(c - 1)
                    make_hi_ahead(c, i)
            with act.Fori(0, 3) as pair:
                for turn in range(2):
                    c = pair * 2 + (C_QK + 2 + turn)
                    for i in range(CK):
                        if i == 0:
                            qk_chunk(c - 1, chunk_bank(C_QK + 1 + turn))
                        if i == 7:
                            qkT_out(c - 1)
                        make_hi_ahead(c, i)

            def exps(tile, buf, n):
                act.wait_ge(neg_max_ready, tile + 1)
                for t, at in enumerate((slice(0, P), slice(P, QB_COLS))):
                    j = 2 * n + t
                    ins = activation(probs[buf][:, at], masked[buf][:, at], ACT.Exp, scale=SCALE,
                                     bias=neg_max[:, j:j + 1], accum_out=sum_p[:, j:j + 1])
                ins.then_inc(probs_ready, 1)

            def probsT_out(head, buf):
                act.wait_ge(probsT_psum, head + 1)
                activation(probsT[buf], ps[:, T0 + buf, 0:QB_COLS], ACT.Copy).then_inc(probsT_ready, 1)

            for c in range(C_V, C_O):
                for i in range(CK):
                    u = c * CK + i
                    if i == 0:
                        if c == C_V:
                            qk_chunk(c - 1, chunk_bank(c - 1))
                        elif c <= C_G:
                            at = (c - 1 - C_V) * CW
                            chunk_to(c - 1, lambda r: v[:, r, at:at + CW])
                        elif c <= C_M:
                            at = (c - 1 - C_G) * CW
                            chunk_to(c - 1, lambda r: g[:, r, at:at + CW], ACT.Silu)
                        else:
                            at = (c - 1 - C_M) * CW
                            chunk_to(c - 1, lambda r: m[:, r, at:at + CW],
                                     ACT.Sigmoid if c == C_O - 1 else ACT.Copy)
                    if c == C_V and i == 7:
                        qkT_out(c - 1)
                    if C_INDEX <= c < C_INDEX + 4 and i % 2 == 0:
                        h = 4 * (c - C_INDEX) + i // 2
                        act.wait_ge(idx_scores, h + 1)
                        if h >= 2:
                            act.wait_ge(idx_added, h - 1)
                        else:
                            act.wait_ge(rope_done, C_V)
                        activation(rel[h % 2], ps[:, S0 + h % 2, 0:QB_COLS], ACT.Relu).then_inc(idx_relu, 1)
                    if U_A <= u < U_B:
                        h, step = divmod(u - U_A, 4)
                        if step == 0:
                            exps(h, h % 2, h % 2)
                        if step == 2:
                            probsT_out(h, h % 2)
                    if U_B <= u < U_OGT:
                        h, step = divmod(u - U_B, 8)
                        if u == U_B:
                            activation(lam_e, lam_s, ACT.Exp).then_inc(lam_exps, 1)
                        if step == 0:
                            for n in range(2):
                                exps(A_HEADS + 2 * h + n, n, n)
                        if step == 4:
                            probsT_out(A_HEADS + h, h % 2)
                        if step == 5:
                            act.wait_ge(heads_psum, A_HEADS + h + 1)
                            for t in range(RT):
                                ins = activation(masked[t][:, 0:2 * HD], ps[:, S0, t * 2 * HD:(t + 1) * 2 * HD],
                                                 ACT.Square, scale=inv_p[:, t:t + 1], accum_out=ss_o[:, t:t + 1])
                            ins.then_inc(o_squares, 1)
                    if u >= U_OGT and i % 2 == 0:
                        n = (u - U_OGT) // 2
                        split_hi_step(8 + n, ogT_hi, 2 * n, T0 + n % 2)
                        if n >= 1 and n <= 6:
                            act.wait_ge(chunk_out, C_M + n)
                            part = m[:, :, (n - 1) * CW:n * CW]
                            activation(part, part, ACT.Sigmoid).then_inc(gates_ready, 1)
                    make_hi_ahead(c, i)

            def merged_hi(t):
                split_hi_step(16 + t, hT_hi, 2 * t, T0 + t % 2)

            for u in range(U_O, U_END):
                if u == U_O:
                    chunk_to(C_O - 1, lambda r: m[:, r, 7 * CW:8 * CW], ACT.Sigmoid)
                n, step = divmod(u - U_O, 8)
                if 1 <= n <= 4 and step in (2, 3):
                    merged_hi(2 * (n - 1) + step - 2)
                if u + RING < U_END:
                    make_hi(u + RING, u % RING, u // RING + 1)

        @block.vector
        def _(dve):
            tt, stt, ts = nc.vector.tensor_tensor, nc.vector.scalar_tensor_tensor, nc.vector.tensor_scalar
            wrote = [0]

            def mark(ins):
                ins.then_inc(dve_wrote, 1)
                wrote[0] = wrote[0] + 1

            def settle():
                dve.wait_ge(dve_wrote, wrote[0])

            def split_lo_step(t, dst, src_hi, k0, bank):
                dve.wait_ge(split_hi, t + 1)
                tt(dst[:, bass.ds(k0, 2), :], ps[:, bank, :].rearrange("p (k s) -> p k s", k=2),
                   src_hi[:, bass.ds(k0, 2), :].bitcast(F32), ALU.subtract).then_inc(split_lo, 1)

            def reduce_phases():
                dve.wait_ge(consts_landed, 11 * 16)
                mark(nc.vector.tensor_copy(pos_f[:, :], pos_i[:, :]))
                mark(tt(lam_prod[:, 0], lams[:, 0], lams[:, 1], ALU.mult))
                mark(tt(lam_prod[:, 1], lams[:, 2], lams[:, 3], ALU.mult))
                settle()
                for r in range(RT):
                    mark(ts(ang[:, r * 64:(r + 1) * 64], freq, pos_f[:, r:r + 1], None, ALU.mult))
                mark(nc.vector.reduce_sum(lam_s, lam_prod, axis=mybir.AxisListType.X))
                settle()
                mark(ts(turns, ang, 1.0 / 6.283185307179586, ROUND, ALU.mult, ALU.add))
                settle()
                mark(ts(red1, turns, ROUND, None, ALU.subtract))
                settle()
                mark(stt(red2, red1, -TWO_PI_1, ang, ALU.mult, ALU.add))
                settle()
                mark(stt(red3, red1, -TWO_PI_2, red2, ALU.mult, ALU.add))
                settle()
                mark(stt(turns, red1, -TWO_PI_3, red3, ALU.mult, ALU.add))
                settle()
                mark(ts(red4, turns, PI_BELOW, -PI_BELOW, ALU.min, ALU.max))
                settle()
                stt(absr, red4, -1.0, red4, ALU.mult, ALU.max).then_inc(reduced, 1)
            def make_tables():
                dve.wait_ge(sin_ready, 2)
                mark(ts(nsin_t, sin_t, -1.0, None, ALU.mult))
                settle()
                half_shape = [P, 4, HD // 2]
                for r in range(RT):
                    c_r, s_r, ns_r = (t[:, r * 64:(r + 1) * 64] for t in (cos_t, sin_t, nsin_t))
                    for b in range(2):
                        half_b, other = slice(b * 64, b * 64 + 64), slice(64 - b * 64, 128 - b * 64)
                        mark(tt(tab_c[:, :, r, half_b], gains[:, :, half_b],
                                c_r.unsqueeze(1).to_broadcast(half_shape), ALU.mult))
                        mark(tt(tab_s[:, :, r, half_b], gains[:, :, other],
                                (ns_r if b == 0 else s_r).unsqueeze(1).to_broadcast(half_shape), ALU.mult))
                        mark(nc.vector.tensor_copy(tab_ci[:, r, b * 32:b * 32 + 32], c_r[:, 0:64:2]))
                        mark(nc.vector.tensor_copy(tab_si[:, r, b * 32:b * 32 + 32],
                                                   (ns_r if b == 0 else s_r)[:, 0:64:2]))
                mark(ts(sub_gain[:, :], sub_gain[:, :], 1.0 - LAMBDA_INIT, None, ALU.mult))

            def x_lo(t):
                dve.wait_ge(split_hi, t + 1)
                for b in range(2):
                    k = 2 * t + b
                    ins = stt(hT_lo[:, k, :], ps[:, 4 + t % 4, b * S:(b + 1) * S], gainT[:, k:k + 1],
                              hT_hi[:, k, :].bitcast(F32), ALU.mult, ALU.subtract)
                ins.then_inc(split_lo, 1)

            def make_lo(u, slot, width=CW):
                dve.wait_ge(hi_ready, u + 1)
                tt(lo[:, slot, :, 0:width], raw[:, slot, :, 0:width], hi[:, slot, :, 0:width].bitcast(F32),
                   ALU.subtract).then_inc(lo_ready, 1)

            def make_lo_ahead(c, i):
                width = chunk_width(c + (i + RING) // CK) if isinstance(c, int) else CW
                make_lo(c * CK + (i + RING), i % RING, width)

            def rope(n, width, cos_of, sin_of, step, cols=CW):
                heads, hw = cols // width, width // 2
                views = [t[:, :, 0:cols].rearrange("p r (h d) -> p r h d", d=width) for t in (stage, roped, swapped)]
                src, cos_out, sin_out = views
                if step == 0:
                    if not isinstance(n, int) or n > 0:
                        dve.wait_ge(qk_transposed, n)
                    for r in range(RT):
                        c_tab = cos_of(r).unsqueeze(1).to_broadcast([P, heads, width])
                        mark(tt(cos_out[:, r], src[:, r], c_tab, ALU.mult))
                        for b in range(2):
                            half_b, other = slice(b * hw, (b + 1) * hw), slice((1 - b) * hw, (2 - b) * hw)
                            s_tab = sin_of(r)[:, half_b].unsqueeze(1).to_broadcast([P, heads, hw])
                            mark(tt(sin_out[:, r, :, half_b], src[:, r, :, other], s_tab, ALU.mult))
                else:
                    settle()
                    tt(roped[:, :, 0:cols], roped[:, :, 0:cols], swapped[:, :, 0:cols],
                       ALU.add).then_inc(rope_done, 1)

            def norm_rope(n, i_tab, step):
                if step == 0:
                    dve.wait_ge(r_h_ready, n - (C_QK - 1))
                    src = stage[:, :, :].rearrange("p r (h d) -> p (r h) d", d=HD)
                    mark(tt(src, src, r_h.unsqueeze(2).to_broadcast([P, 8, HD]), ALU.mult))
                elif step == 1:
                    settle()
                    rope(n, HD, lambda r: tab_c[:, bass.ds(i_tab, 1), r, :].squeeze(1),
                         lambda r: tab_s[:, bass.ds(i_tab, 1), r, :].squeeze(1), 0)
                else:
                    rope(n, HD, None, None, 1)

            def index_rope(n, step):
                if step == 0:
                    dve.wait_ge(chunk_out, n + 1)
                    settle()
                if n == C_QK - 1 and step == 0:
                    mark(tt(k_cos, kst[:, :, 0:IDX_DIM], tab_ci, ALU.mult))
                    for b in range(2):
                        half_b, other = slice(b * 32, b * 32 + 32), slice(32 - b * 32, 64 - b * 32)
                        mark(tt(k_swap[:, :, half_b], kst[:, :, other], tab_si[:, :, half_b], ALU.mult))
                    mark(ts(w_idx[:, :, :], kst[:, :, IDX_DIM:KIWI], IDX_SCALE, None, ALU.mult))
                if n == C_QK - 1 and step == 1:
                    settle()
                    for b in range(2):
                        mark(tt(kr[:, :, b * IDX_DIM:(b + 1) * IDX_DIM], k_cos, k_swap, ALU.add))
                rope(n, IDX_DIM, lambda r: tab_ci[:, r, :], lambda r: tab_si[:, r, :], step, IDX_BLOCKS[n] * P)

            for u in range(CK):
                x_lo(u)
                make_lo(u, u % RING, IDX_W[0])
            for i in range(4, CK):
                if i == 5:
                    reduce_phases()
                if i == 7:
                    make_tables()
                make_lo_ahead(0, i)
            for c in range(1, C_QK + 2):
                for i in range(CK):
                    if c <= C_QK and 1 <= i <= 2:
                        index_rope(c - 1, i - 1)
                    if c == C_QK + 1 and 1 <= i <= 3:
                        norm_rope(c - 1, 0, i - 1)
                    make_lo_ahead(c, i)
            before = wrote[0]
            for_each = 2 * (1 + 6)
            with dve.Fori(0, 3) as pair:
                wrote[0] = pair * for_each + before
                for turn in range(2):
                    c = pair * 2 + (C_QK + 2 + turn)
                    for i in range(CK):
                        if 1 <= i <= 3:
                            norm_rope(c - 1, pair + turn, i - 1)
                        make_lo_ahead(c, i)
            wrote[0] = before + 3 * for_each

            def masked_max(buf, bank, bias, n, tile):
                dve.wait_ge(scores, tile + 1)
                for t, at in enumerate((slice(0, P), slice(P, QB_COLS))):
                    j = 2 * n + t
                    mark(nc.vector.tensor_tensor_reduce(
                        out=masked[buf][:, at], in0=ps[:, bank, at], in1=bias[:, at], scale=1.0, scalar=MARK,
                        op0=ALU.add, op1=ALU.max, accum_out=max_s[:, j:j + 1]))
                settle()
                ts(neg_max[:, 2 * n:2 * n + 2], max_s[:, 2 * n:2 * n + 2], -SCALE, None,
                   ALU.mult).then_inc(neg_max_ready, 1)

            def topk_round():
                tiles = (slice(0, P), slice(P, QB_COLS))
                settle()
                for t, at in enumerate(tiles):
                    mark(nc.vector.max(top8[:, t], score[:, at]))
                settle()
                for t, at in enumerate(tiles):
                    mark(nc.vector.match_replace(score[:, at], top8[:, t], score[:, at], MARK))

            for c in range(C_V, C_O):
                for i in range(CK):
                    u = c * CK + i
                    if c == C_V and 1 <= i <= 3:
                        norm_rope(c - 1, 3, i - 1)
                    if C_INDEX <= c < C_INDEX + 4 and i % 2 == 0:
                        h = 4 * (c - C_INDEX) + i // 2
                        if h == 0:
                            dve.wait_ge(causal_ready, 1)
                        dve.wait_ge(idx_relu, h + 1)
                        settle()
                        for t, at in enumerate((slice(0, P), slice(P, QB_COLS))):
                            ins = stt(score[:, at], rel[h % 2][:, at], w_idx[:, t, h:h + 1],
                                      (bias_b if h == 0 else score)[:, at], ALU.mult, ALU.add)
                            if t == 0:
                                mark(ins)
                        ins.then_inc(idx_added, 1)
                        dve.wait_ge(idx_added, h + 1)
                    if c == U_TOPK // CK:
                        topk_round()
                    if u == U_A - 1:
                        settle()
                        mark(ts(bias_a[:, :], score[:, :], 0.5 * MARK, NEG, ALU.is_gt, ALU.mult))
                        settle()
                        mark(tt(bias_a[:, :], bias_a[:, :], bias_b[:, :], ALU.add))
                        settle()
                    if U_A <= u < U_B:
                        h, step = divmod(u - U_A, 4)
                        n = h % 2
                        if step == 0:
                            masked_max(n, S0 + n, bias_a, n, h)
                        if step == 3:
                            dve.wait_ge(probs_ready, h + 1)
                            mark(nc.vector.reciprocal(inv_p[:, 2 * n:2 * n + 2], sum_p[:, 2 * n:2 * n + 2]))
                            dve.wait_ge(heads_psum, h + 1)
                            dve.wait_ge(chunk_out, C_G + 2)
                            settle()
                            for t in range(RT):
                                part = g[:, t, h * HD:(h + 1) * HD]
                                ins = stt(part, ps[:, S0 + n, t * HD:(t + 1) * HD], inv_p[:, 2 * n + t:2 * n + t + 1],
                                          part, ALU.mult, ALU.mult)
                            ins.then_inc(og_ready, 1)
                    if c == C_M and i in (1, 2):
                        r = i - 1
                        if r == 0:
                            dve.wait_ge(chunk_out, C_M)
                        part = g[:, r, A_W:2 * A_W].rearrange("p (h d) -> p h d", d=2 * HD)
                        mark(tt(part, part, sub_gain[:, :].unsqueeze(1).to_broadcast([P, B_HEADS, 2 * HD]), ALU.mult))
                    if U_B <= u < U_OGT:
                        h, step = divmod(u - U_B, 8)
                        if step == 0:
                            for n in range(2):
                                masked_max(n, S0 + n, bias_b, n, A_HEADS + 2 * h + n)
                        if step == 2:
                            dve.wait_ge(probs_ready, A_HEADS + 2 * h + 2)
                            mark(nc.vector.reciprocal(inv_p, sum_p))
                            if h == 0:
                                dve.wait_ge(lam_exps, 1)
                                mark(stt(neg_lam, lam_e[:, 1:2], -LAMBDA_INIT, lam_e[:, 0:1],
                                         ALU.add, ALU.subtract))
                            settle()
                            mark(stt(mix, sum_p[:, 0:2], neg_lam, inv_p[:, 2:4], ALU.mult, ALU.mult))
                            settle()
                            for t, at in enumerate((slice(0, P), slice(P, QB_COLS))):
                                ins = stt(probs[0][:, at], probs[1][:, at], mix[:, t:t + 1], probs[0][:, at],
                                          ALU.mult, ALU.add)
                            ins.then_inc(mixed, 1)
                        if step == 6:
                            dve.wait_ge(r_o_ready, h + 1)
                            mark(tt(f_o, r_o, inv_p[:, 0:2], ALU.mult))
                            settle()
                            for t in range(RT):
                                at = A_W + h * 2 * HD
                                part = g[:, t, at:at + 2 * HD]
                                ins = stt(part, ps[:, S0, t * 2 * HD:(t + 1) * 2 * HD], f_o[:, t:t + 1], part,
                                          ALU.mult, ALU.mult)
                            ins.then_inc(og_ready, 1)
                    if u >= U_OGT and i % 2 == 0:
                        n = (u - U_OGT) // 2
                        split_lo_step(8 + n, ogT_lo, ogT_hi, 2 * n, T0 + n % 2)
                    make_lo_ahead(c, i)

            def add_residual(u, n):
                dve.wait_ge(unit_done, u)
                if n == 0:
                    dve.wait_ge(res_landed, 16)
                part = g[:, :, n * CW:(n + 1) * CW]
                bank = 2 * (n % 2)
                tt(part, ps[:, bank:bank + 2, :], part, ALU.add).then_inc(tail_out, 1)

            for u in range(U_O, U_END):
                n, step = divmod(u - U_O, 8)
                if n < 4 and step == 4:
                    if n == 0:
                        dve.wait_ge(gates_ready, 6)
                        dve.wait_ge(chunk_out, C_O)
                    dve.wait_ge(unit_done, u)
                    part = m[:, :, n * CW:(n + 1) * CW]
                    tt(part, ps[:, 0:2, :], part, ALU.mult).then_inc(tail_out, 1)
                if 1 <= n <= 4 and step == 0:
                    dve.wait_ge(unit_done, u)
                    a_part, b_part = (m[:, :, b * D + (n - 1) * CW:b * D + n * CW] for b in range(2))
                    tt(b_part, ps[:, 2:4, :], b_part, ALU.mult).then_inc(tail_out, 1)
                    dve.wait_ge(tail_out, 2 * n)
                    if n >= 2:
                        dve.wait_ge(split_T, 16 + 2 * (n - 1))
                    tt(stage[:, :, :], a_part, b_part, ALU.add).then_inc(merged, 1)
                if 1 <= n <= 4 and step in (2, 3):
                    t = 2 * (n - 1) + step - 2
                    split_lo_step(16 + t, hT_lo, hT_hi, 2 * t, T0 + t % 2)
                if u >= U_W + CK and step == 0:
                    add_residual(u, n - 5)
                if u + RING < U_END:
                    make_lo(u + RING, u % RING)
            for r in range(RT):
                if r == 0:
                    dve.wait_ge(last_rows, 1)
                else:
                    dve.wait_ge(unit_done, U_END)
                part = g[:, r, 3 * CW:4 * CW]
                tt(part, ps[:, 2 + r, :], part, ALU.add).then_inc(tail_out, 1)


_INS = ["x", "positions", "inv_freq", "norm_gain", "w_in", "a_q_gain", "a_k_gain", "b_q_gain", "b_k_gain",
        "lambda_q1", "lambda_k1", "lambda_q2", "lambda_k2", "b_subln_gain", "w_o_a", "w_o_b", "w_out"]


def kernel(**inputs):
    import numpy as _np
    import concourse.bacc as _bacc
    from concourse import mybir as _mybir
    from concourse.bass_utils import run_bass_kernel_spmd as _run

    exponents = _np.arange(0, HD, 2, dtype=_np.float32) / _np.float32(HD)
    freqs = (_np.float32(10000.0) ** -exponents).astype(_np.float32)[None]

    nc = _bacc.Bacc("TRN2", target_bir_lowering=False, num_devices=1)
    arrays, args = {}, []
    for name in _INS:
        a = freqs if name == "inv_freq" else _np.ascontiguousarray(inputs[name])
        arrays[f"in_{name}"] = a
        args.append(nc.dram_tensor(f"in_{name}", a.shape, _mybir.dt.from_np(a.dtype), kind="ExternalInput").ap())
    args.append(nc.dram_tensor("out_0", (1, S, D), _mybir.dt.from_np(_np.dtype("float32")),
                               kind="ExternalOutput").ap())
    build_layer(nc, *args)
    return _run(nc, [arrays], core_ids=[0]).results[0]["out_0"]
```

```python
from contextlib import ExitStack

import concourse.bass as bass
from concourse import mybir
from concourse.alu_op_type import AluOpType as ALU

ACT = mybir.ActivationFunctionType
F32 = mybir.dt.float32
F32R = mybir.dt.float32r
I32 = mybir.dt.int32

P = 128
D = 2048
S = 256
RT = S // P
KT = D // P
HD = 128
IDX_HEADS, IDX_DIM = 16, 64
TOPK = S // 4
A_HEADS, B_HEADS = 8, 4
NORM_EPS, SUBLN_EPS = 1e-6, 1e-5
LAMBDA_INIT = 0.2
SCALE = HD ** -0.5
IDX_SCALE = IDX_HEADS ** -0.5 * IDX_DIM ** -0.5

CW = 512
X_CUTS = (0, 256, 512, 1024, 1536, 2048)
CK = 8
RING = 4
WARM_UP = (6, 2)
KIWI = IDX_DIM + IDX_HEADS
IDX_W = (384, 384, 256 + KIWI)
IDX_BLOCKS = tuple(w // P for w in IDX_W)
A_W = A_HEADS * HD

COL = {}
_at = 0
for _name, _width in (("qa", A_W), ("ka", A_W), ("va", A_W), ("ga", A_W), ("qi", A_W), ("kiwi", KIWI),
                      ("qb", A_W), ("kb", A_W), ("vb", A_W), ("gb", A_W), ("ma", D), ("mb", D)):
    COL[_name] = _at
    _at += _width
IN_COLS = _at

C_QK, C_V, C_G, C_M = 3, 11, 15, 19
C_O = 27
U_O = C_O * CK
U_W = U_O + 8 * 4
U_END = U_W + 4 * CK
C_INDEX = C_V + 1
U_TOPK = (C_INDEX + 4) * CK
U_A = U_TOPK + CK
U_B = U_A + 4 * A_HEADS
U_OGT = U_B + 8 * B_HEADS
assert U_OGT + 16 == U_O

NEG = -1.0e30
MARK = -3.0e38
TWO_PI_1 = 6.28125
TWO_PI_2 = 0.0019350051879882812
TWO_PI_3 = 3.0199159819e-07
ROUND = 12582912.0
PI_BELOW = 3.1415925
HALF_PI = 1.5707963267948966


def chunk_width(c):
    return IDX_W[c] if c < C_QK else CW


def chunk_bank(c):
    return 2 * ((c + 1) % 2)


def build_layer(nc, x, positions, inv_freq, norm_gain, w_in, a_q_gain, a_k_gain, b_q_gain, b_k_gain,
                lambda_q1, lambda_k1, lambda_q2, lambda_k2, b_subln_gain, w_o_a, w_o_b, w_out, out):
    x_rows = x[0].rearrange("(r p) d -> p r d", p=P)
    out_rows = out[0].rearrange("(r p) d -> p r d", p=P)

    with ExitStack() as ctx:
        place = [-(-nc.sbuf_base // 64) * 64]

        def sb(name, shape, dt=F32, at=None):
            size = 4
            for n in shape[1:]:
                size *= n
            offset = place[0] if at is None else at
            if at is None:
                place[0] += -(-size // 64) * 64
                assert place[0] <= nc.sbuf_usable_end, (name, place[0])
            return nc.alloc_sbuf_tensor_at(name, shape, dt, offset=offset)

        def sem(name):
            return ctx.enter_context(nc.semaphore(name))

        raw = sb("raw", [P, RING, 2, CW])
        hi = sb("hi", [P, RING, 2, CW], F32R)
        lo = sb("lo", [P, RING, 2, CW], F32R)
        hT_hi = sb("hT_hi", [P, KT, S], F32R)
        hT_lo = sb("hT_lo", [P, KT, S], F32R)
        qk_at = place[0]
        qkT = sb("qkT", [P, 5 * 8, S])
        ogT_hi = sb("ogT_hi", [P, KT, S], F32R, at=qk_at)
        ogT_lo = sb("ogT_lo", [P, KT, S], F32R, at=qk_at + 4 * KT * S)
        QI, QA, KA, QB, KB = 0, 8, 16, 24, 32
        v = sb("v", [P, RT, 2 * A_W])
        g = sb("g", [P, RT, 2 * A_W])
        m = sb("m", [P, RT, 2 * D])
        xr = m[:, 0, :].rearrange("p (r d) -> p r d", r=RT)

        ident = sb("ident", [P, P])
        stage = sb("stage", [P, RT, CW])
        roped = sb("roped", [P, RT, CW])
        swapped = sb("swapped", [P, RT, CW])
        QB_COLS = 3 * P
        work_flat = [stage[:, :, :].rearrange("p r n -> p (r n)"),
                     roped[:, :, :].rearrange("p r n -> p (r n)"),
                     swapped[:, :, :].rearrange("p r n -> p (r n)")]
        masked = [work_flat[0][:, i * QB_COLS:(i + 1) * QB_COLS] for i in range(2)]
        probs = [work_flat[1][:, i * QB_COLS:(i + 1) * QB_COLS] for i in range(2)]
        probsT = [work_flat[2][:, i * QB_COLS:(i + 1) * QB_COLS] for i in range(2)]
        rel = masked
        score = sb("score", [P, QB_COLS])
        bias_a = sb("bias_a", [P, QB_COLS])
        bias_b = sb("bias_b", [P, QB_COLS])
        kiT = sb("kiT", [P, S])
        w_idx = sb("w_idx", [P, RT, IDX_HEADS])
        sub_gain = sb("sub_gain", [P, 2 * HD])
        gain_rows = sb("gain_rows", [KT, P])
        gainT = sb("gainT", [P, KT])
        top8 = sb("top8", [P, 2, 8])
        pos_i = sb("pos_i", [P, RT], I32)
        pos_f = sb("pos_f", [P, RT])
        half = sb("half", [P, 8])
        small = sb("small", [P, 96])
        ss_x, ms_x, rstd = small[:, 0:2], small[:, 2:4], small[:, 4:6]
        ss_h, ms_h, r_h = small[:, 8:16], small[:, 16:24], small[:, 24:32]
        lam_s, lam_e, neg_lam = small[:, 32:34], small[:, 34:36], small[:, 36:37]
        max_s, neg_max, sum_p = small[:, 40:44], small[:, 44:48], small[:, 48:52]
        inv_p, mix = small[:, 52:56], small[:, 56:58]
        ss_o, ms_o, r_o, f_o = small[:, 60:62], small[:, 62:64], small[:, 64:66], small[:, 66:68]

        v0 = v[:, 0, :]
        gains = v0[:, 0:512].rearrange("p (i d) -> p i d", i=4)
        lams = v0[:, 512:1024].rearrange("p (i d) -> p i d", i=4)
        lam_prod = v0[:, 1024:1280].rearrange("p (i d) -> p i d", i=2)
        v1 = v[:, 1, :]
        freq = v1[:, 0:64]

        def phases(n):
            return v1[:, 64 + 128 * n:192 + 128 * n]

        ang, turns, red1, red2, red3, red4, absr, sin_t, cos_t, nsin_t = (phases(n) for n in range(10))
        kst = v1[:, 1408:1568].rearrange("p (r n) -> p r n", r=RT)
        k_cos = v1[:, 1568:1696].rearrange("p (r n) -> p r n", r=RT)
        k_swap = v1[:, 1696:1824].rearrange("p (r n) -> p r n", r=RT)
        kr = v0[:, 1280:1536].rearrange("p (r n) -> p r n", r=RT)
        tab_c = g[:, 0, 0:1024].rearrange("p (i r d) -> p i r d", i=4, r=RT)
        tab_s = g[:, 0, 1024:2048].rearrange("p (i r d) -> p i r d", i=4, r=RT)
        tab_ci = g[:, 1, 0:128].rearrange("p (r d) -> p r d", r=RT)
        tab_si = g[:, 1, 128:256].rearrange("p (r d) -> p r d", r=RT)

        ps = ctx.enter_context(nc.psum_tensor("ps", [P, 8, CW], F32))
        T0, S0 = 4, 6

        x_landed = [sem(f"x_landed_{i}") for i in range(len(X_CUTS) - 1)]
        consts_landed = sem("consts_landed")
        gain_landed = sem("gain_landed")
        raw_landed = [sem(f"raw_landed_{i}") for i in range(RING)]
        res_landed = sem("res_landed")
        out_landed = sem("out_landed")
        ident_ready = sem("ident_ready")
        causal_ready = sem("causal_ready")
        pool_wrote = sem("pool_wrote")
        hi_ready, lo_ready, unit_done = sem("hi_ready"), sem("lo_ready"), sem("unit_done")
        chunk_out, tail_out = sem("chunk_out"), sem("tail_out")
        split_T, split_hi, split_lo = sem("split_T"), sem("split_hi"), sem("split_lo")
        gainT_psum, gainT_ready = sem("gainT_psum"), sem("gainT_ready")
        reduced, sin_ready = sem("reduced"), sem("sin_ready")
        index_tables_ready, tables_ready = sem("index_tables_ready"), sem("tables_ready")
        lam_sums, lam_exps = sem("lam_sums"), sem("lam_exps")
        x_squares, rstd_ready = sem("x_squares"), sem("rstd_ready")
        h_squares, r_h_ready, rope_done = sem("h_squares"), sem("r_h_ready"), sem("rope_done")
        qk_transposed, qkT_ready = sem("qk_transposed"), sem("qkT_ready")
        idx_scores, idx_relu, idx_added = sem("idx_scores"), sem("idx_relu"), sem("idx_added")
        scores, neg_max_ready, probs_ready = sem("scores"), sem("neg_max_ready"), sem("probs_ready")
        probsT_psum, probsT_ready, heads_psum, og_ready = (sem("probsT_psum"), sem("probsT_ready"),
                                                           sem("heads_psum"), sem("og_ready"))
        mixed = sem("mixed")
        o_squares, r_o_ready = sem("o_squares"), sem("r_o_ready")
        gates_ready = sem("gates_ready")
        merged = sem("merged")
        last_rows = sem("last_rows")
        dve_wrote = sem("dve_wrote")

        block = ctx.enter_context(nc.Block())

        @block.sync
        def _(sp):
            def load_x(j):
                at = slice(X_CUTS[j], X_CUTS[j + 1])
                sp.dma_start(xr[:, :, at], x_rows[:, :, at]).then_inc(x_landed[j], 16)

            def load(slot, u, weights, k0, col, width=CW):
                if not isinstance(u, int) or u >= RING:
                    sp.wait_ge(lo_ready, u - (RING - 1))
                src = weights[0][k0 * P:(k0 + 2) * P, bass.ds(col, width)].rearrange("(k p) n -> p k n", p=P)
                sp.dma_start(raw[:, slot, :, 0:width], src).then_inc(raw_landed[slot], 16)

            def load_chunk(c, col, width=CW):
                for i in range(CK):
                    load(i % RING, c * CK + i, w_in, 2 * i, col, width)

            for i in range(CK):
                if i <= 3:
                    load_x(i)
                if i == 3:
                    load_x(4)
                if i == 4:
                    sp.dma_start(pos_i[:, :], positions[0].rearrange("(r p) -> p r", p=P),
                                  allow_slow_non_contiguous=True).then_inc(consts_landed, 16)
                    sp.dma_start(freq, inv_freq[0].partition_broadcast(P)).then_inc(consts_landed, 16)
                    for j, row in enumerate((a_q_gain, a_k_gain, b_q_gain, b_k_gain)):
                        sp.dma_start(gains[:, j], row[0].partition_broadcast(P)).then_inc(consts_landed, 16)
                    for j, row in enumerate((lambda_q1, lambda_k1, lambda_q2, lambda_k2)):
                        sp.dma_start(lams[:, j], row[0].partition_broadcast(P)).then_inc(consts_landed, 16)
                    sp.dma_start(sub_gain[:, :], b_subln_gain[0].partition_broadcast(P)).then_inc(consts_landed, 16)
                load(i % RING, i, w_in, 2 * i, COL["qi"], IDX_W[0])
            load_chunk(1, COL["qi"] + IDX_W[0], IDX_W[1])
            load_chunk(2, COL["qi"] + IDX_W[0] + IDX_W[1], IDX_W[2])
            with sp.Fori(0, 2) as branch:
                with sp.Fori(0, 4) as n:
                    load_chunk(C_QK + branch * 4 + n, branch * COL["qb"] + n * CW)
            for c, name in ((C_V, "va"), (C_V + 2, "vb"), (C_G, "ga"), (C_G + 2, "gb")):
                with sp.Fori(0, 2) as n:
                    load_chunk(n + c, n * CW + COL[name])
            with sp.Fori(0, 8) as n:
                load_chunk(n + C_M, n * CW + COL["ma"])

            def load_projections(n):
                for b, weights in enumerate((w_o_a, w_o_b)):
                    for i in range(4):
                        load(i, n * 8 + (U_O + 4 * b + i), weights, 2 * i, n * CW)

            load_projections(0)
            sp.wait_ge(split_lo, 16)
            sp.dma_start(g[:, :, :], x_rows).then_inc(res_landed, 16)
            with sp.Fori(1, 4) as n:
                load_projections(n)
            with sp.Fori(0, 4) as n:
                for i in range(CK):
                    load(i % RING, n * CK + (U_W + i), w_out, 2 * i, n * CW)
            for n in range(3):
                sp.wait_ge(tail_out, 8 + n + 1)
                sp.dma_start(out_rows[:, :, n * CW:(n + 1) * CW],
                             g[:, :, n * CW:(n + 1) * CW]).then_inc(out_landed, 16)
            for r in range(RT):
                sp.wait_ge(tail_out, 11 + r + 1)
                sp.dma_start(out_rows[:, r, 3 * CW:4 * CW], g[:, r, 3 * CW:4 * CW]).then_inc(out_landed, 16)
            sp.wait_ge(out_landed, 5 * 16)

        @block.gpsimd
        def _(pool):
            nc.gpsimd.memset(ident[:, :], 0.0).then_inc(pool_wrote, 1)
            nc.gpsimd.memset(bias_b[:, :], 0.0).then_inc(pool_wrote, 1)
            nc.gpsimd.memset(half[:, :], -0.5).then_inc(pool_wrote, 1)
            pool.wait_ge(pool_wrote, 3)
            nc.gpsimd.affine_select(out=ident[:, :], in_=ident[:, :], compare_op=ALU.not_equal, fill=1.0,
                                    base=0, pattern=[[-1, P]], channel_multiplier=1).then_inc(ident_ready, 1)
            for start in (0, 2 * P):
                blk = bias_b[:, start:start + P]
                last = nc.gpsimd.affine_select(out=blk, in_=blk, compare_op=ALU.is_ge, fill=NEG, base=0,
                                               pattern=[[-1, P]], channel_multiplier=1)
            last.then_inc(causal_ready, 1)
            wrote = [3]

            def mark(ins):
                ins.then_inc(pool_wrote, 1)
                wrote[0] = wrote[0] + 1

            def settle():
                pool.wait_ge(pool_wrote, wrote[0])

            tt, ts = nc.gpsimd.tensor_tensor, nc.gpsimd.tensor_scalar

            def root(out, mean, total, n, width, eps):
                mark(ts(mean, total, 1.0 / n, eps, ALU.mult, ALU.add))
                settle()
                return tt(out, mean, half[:, 0:width], ALU.pow)

            pool.wait_ge(consts_landed, 11 * 16)
            mark(nc.gpsimd.tensor_copy(pos_f[:, :], pos_i[:, :]))
            settle()
            for r in range(RT):
                mark(ts(ang[:, r * 64:(r + 1) * 64], freq, pos_f[:, r:r + 1], None, ALU.mult))
            settle()
            mark(ts(turns, ang, 1.0 / 6.283185307179586, ROUND, ALU.mult, ALU.add))
            settle()
            mark(ts(red1, turns, ROUND, None, ALU.subtract))
            settle()
            for source, part, left in ((ang, TWO_PI_1, red2), (red2, TWO_PI_2, red3), (red3, TWO_PI_3, red4)):
                mark(ts(turns, red1, -part, None, ALU.mult))
                settle()
                mark(tt(left, turns, source, ALU.add))
                settle()
            mark(ts(ang, red4, PI_BELOW, -PI_BELOW, ALU.min, ALU.max))
            settle()
            mark(ts(turns, ang, 0.0, None, ALU.max))
            mark(ts(red1, ang, 0.0, None, ALU.min))
            settle()
            tt(absr, turns, red1, ALU.subtract).then_inc(reduced, 1)

            pool.wait_ge(x_squares, 1)
            root(rstd, ms_x, ss_x, D, RT, NORM_EPS).then_inc(rstd_ready, 1)

            pool.wait_ge(sin_ready, 2)
            mark(ts(nsin_t, sin_t, -1.0, None, ALU.mult))
            settle()
            rows = [[t[:, r * 64:(r + 1) * 64] for t in (cos_t, nsin_t, sin_t)] for r in range(RT)]
            for r, (c_r, *s_r) in enumerate(rows):
                for b in range(2):
                    half_b = slice(b * 32, b * 32 + 32)
                    nc.gpsimd.tensor_copy(tab_ci[:, r, half_b], c_r[:, 0:64:2]).then_inc(index_tables_ready, 1)
                    nc.gpsimd.tensor_copy(tab_si[:, r, half_b], s_r[b][:, 0:64:2]).then_inc(index_tables_ready, 1)
            half_shape = [P, 4, HD // 2]
            for r, (c_r, *s_r) in enumerate(rows):
                for b in range(2):
                    half_b, other = slice(b * 64, b * 64 + 64), slice(64 - b * 64, 128 - b * 64)
                    tt(tab_c[:, :, r, half_b], gains[:, :, half_b],
                       c_r.unsqueeze(1).to_broadcast(half_shape), ALU.mult).then_inc(tables_ready, 1)
                    tt(tab_s[:, :, r, half_b], gains[:, :, other],
                       s_r[b].unsqueeze(1).to_broadcast(half_shape), ALU.mult).then_inc(tables_ready, 1)
            ts(sub_gain[:, :], sub_gain[:, :], 1.0 - LAMBDA_INIT, None, ALU.mult).then_inc(tables_ready, 1)

            for n in range(8):
                pool.wait_ge(h_squares, n + 1)
                root(r_h, ms_h, ss_h, HD, 8, NORM_EPS).then_inc(r_h_ready, 1)
            for h in range(B_HEADS):
                pool.wait_ge(o_squares, h + 1)
                root(r_o, ms_o, ss_o, 2 * HD, RT, SUBLN_EPS).then_inc(r_o_ready, 1)

        @block.tensor
        def _(pe):
            mm = nc.tensor.matmul

            def unit(u, slot, k0, s_hi, s_lo, bank, first, last, width=CW, rows_done=None):
                w_hi, w_lo = (t[:, slot, :, 0:width] for t in (hi, lo))
                pe.wait_ge(lo_ready, u + 1)
                order = [(j, r) for j in range(2) for r in range(RT)]
                if rows_done is not None:
                    order.sort(key=lambda jr: jr[1])
                for j, r in order:
                    a_hi = s_hi[:, k0 + j, r * P:(r + 1) * P]
                    a_lo = s_lo[:, k0 + j, r * P:(r + 1) * P]
                    o = ps[:, bank + r, 0:width]
                    mm(o, a_hi, w_hi[:, j], start=first and j == 0, stop=False)
                    mm(o, a_hi, w_lo[:, j], start=False, stop=False)
                    ins = mm(o, a_lo, w_hi[:, j], start=False, stop=last and j == 1)
                    if rows_done is not None and j == 1 and r == 0:
                        ins.then_inc(rows_done, 1)
                ins.then_inc(unit_done, 1)

            def first_unit():
                tiles = [(j, r) for j in range(2) for r in range(RT)]
                for parts, operand, part in ((hi_ready, hT_hi, hi), (hi_ready, hT_lo, hi), (lo_ready, hT_hi, lo)):
                    pe.wait_ge(parts, 1)
                    for j, r in tiles:
                        ins = mm(ps[:, chunk_bank(0) + r, 0:IDX_W[0]], operand[:, j, r * P:(r + 1) * P],
                                 part[:, 0, j, 0:IDX_W[0]], start=part is hi and operand is hT_hi and j == 0,
                                 stop=False)
                ins.then_inc(unit_done, 1)

            def w_in_unit(c, i, bank, width=CW):
                if isinstance(c, int) and c == 0:
                    pe.wait_ge(split_lo, i + 1)
                    if i == 0:
                        first_unit()
                        return
                if i == 0 and (not isinstance(c, int) or c >= 2):
                    pe.wait_ge(chunk_out, c - 1)
                unit(c * CK + i, i % RING, 2 * i, hT_hi, hT_lo, bank, i == 0, i == CK - 1, width)

            def transpose_roped(n, blocks=4):
                pe.wait_ge(rope_done, n + 1)
                if not isinstance(n, int) or n > 0:
                    pe.wait_ge(qkT_ready, n)
                for b in range(blocks):
                    for r in range(RT):
                        o = ps[:, T0 + b // 2, (b % 2) * S + r * P:(b % 2) * S + (r + 1) * P]
                        ins = nc.tensor.transpose(o, roped[:, r, b * P:(b + 1) * P], ident[:, :])
                if isinstance(n, int) and n == C_QK - 1:
                    for r in range(RT):
                        ins = nc.tensor.transpose(ps[:, T0 + 1, r * P:(r + 1) * P], kr[:, r, :], ident[:, :])
                ins.then_inc(qk_transposed, 1)

            def transpose_step(rows, bank):
                for b in range(2):
                    for r in range(RT):
                        o = ps[:, bank, b * S + r * P:b * S + (r + 1) * P]
                        ins = nc.tensor.transpose(o, rows(b, r), ident[:, :])
                ins.then_inc(split_T, 1)

            def warm_up(count):
                for _ in range(count):
                    mm(ps[:, S0 + 1, 0:P], ident[:, :], ident[:, :], start=True, stop=True)

            pe.wait_ge(ident_ready, 1)
            warm_up(WARM_UP[0])
            pe.wait_ge(gain_landed, 16)
            nc.tensor.transpose(ps[:, 0, 0:KT], gain_rows[:, :], ident[0:KT, 0:KT]).then_inc(gainT_psum, 1)

            def transpose_x(n):
                if 256 * n in X_CUTS:
                    pe.wait_ge(x_landed[X_CUTS.index(256 * n)], 16)
                if n >= 4:
                    pe.wait_ge(split_lo, n - 3)
                transpose_step(lambda b, r: xr[:, r, (2 * n + b) * P:(2 * n + b + 1) * P], 4 + n % 4)

            transpose_x(0)
            transpose_x(1)
            warm_up(WARM_UP[1])
            for c in range(C_QK + 2):
                for i in range(CK):
                    if c == 0 and i in (1, 2, 3):
                        transpose_x(2 * i)
                        transpose_x(2 * i + 1)
                    if c == 1 and i == 0:
                        pe.wait_ge(gainT_ready, 1)
                    if c == 1 and i == 6:
                        pe.wait_ge(split_lo, 8)
                    if c >= 1 and i == 6:
                        transpose_roped(c - 1, IDX_BLOCKS[c - 1] if c <= C_QK else 4)
                    w_in_unit(c, i, chunk_bank(c), chunk_width(c))
            with pe.Fori(0, 3) as pair:
                for turn in range(2):
                    c = pair * 2 + (C_QK + 2 + turn)
                    for i in range(CK):
                        if i == 6:
                            transpose_roped(c - 1)
                        w_in_unit(c, i, chunk_bank(C_QK + 2 + turn))

            def index_scores(h):
                if h < 2:
                    pe.wait_ge(qkT_ready, C_QK)
                else:
                    pe.wait_ge(idx_relu, h - 1)
                a = (h % 2) * IDX_DIM
                q = qkT[a:a + IDX_DIM, QI + h // 2, :]
                k = kiT[a:a + IDX_DIM, :]
                o = ps[:, S0 + h % 2, :]
                mm(o[:, 0:P], q[:, 0:P], k[:, 0:P], start=True, stop=True)
                mm(o[:, P:P + S], q[:, P:S], k[:, :], start=True, stop=True).then_inc(idx_scores, 1)

            def qk_scores(q_block, k_block, bank):
                o = ps[:, bank, :]
                mm(o[:, 0:P], qkT[:, q_block, 0:P], qkT[:, k_block, 0:P], start=True, stop=True)
                mm(o[:, P:P + S], qkT[:, q_block, P:S], qkT[:, k_block, :],
                   start=True, stop=True).then_inc(scores, 1)

            def transpose_probs(src, head):
                for b in range(3):
                    ins = nc.tensor.transpose(ps[:, T0 + head % 2, b * P:(b + 1) * P],
                                              src[:, b * P:(b + 1) * P], ident[:, :])
                ins.then_inc(probsT_psum, 1)

            def weighted_values(pT, bank, col, width):
                o = ps[:, bank, :]
                mm(o[:, 0:width], pT[:, 0:P], v[:, 0, col:col + width], start=True, stop=True)
                mm(o[:, width:2 * width], pT[:, P:2 * P], v[:, 0, col:col + width], start=True, stop=False)
                mm(o[:, width:2 * width], pT[:, 2 * P:3 * P], v[:, 1, col:col + width],
                   start=False, stop=True).then_inc(heads_psum, 1)

            for c in range(C_V, C_O):
                for i in range(CK):
                    u = c * CK + i
                    if c == C_V and i == 6:
                        transpose_roped(C_V - 1)
                    if C_INDEX <= c < C_INDEX + 4 and i % 2 == 0:
                        index_scores(4 * (c - C_INDEX) + i // 2)
                    if U_A <= u < U_B:
                        h, step = divmod(u - U_A, 4)
                        if step == 0:
                            if h < 2:
                                pe.wait_ge(idx_relu, IDX_HEADS)
                                pe.wait_ge(qkT_ready, C_V)
                            else:
                                pe.wait_ge(og_ready, h - 1)
                            qk_scores(QA + h, KA + h, S0 + h % 2)
                        if step == 2:
                            pe.wait_ge(probs_ready, h + 1)
                            transpose_probs(probs[h % 2], h)
                        if step == 3:
                            pe.wait_ge(probsT_ready, h + 1)
                            weighted_values(probsT[h % 2], S0 + h % 2, h * HD, HD)
                    if U_B <= u < U_OGT:
                        h, step = divmod(u - U_B, 8)
                        if step == 0:
                            pe.wait_ge(og_ready, A_HEADS + h)
                            for n in range(2):
                                qk_scores(QB + 2 * h + n, KB + 2 * h + n, S0 + n)
                        if step == 4:
                            pe.wait_ge(mixed, h + 1)
                            transpose_probs(probs[0], h)
                        if step == 5:
                            pe.wait_ge(probsT_ready, A_HEADS + h + 1)
                            weighted_values(probsT[h % 2], S0, A_W + 2 * h * HD, 2 * HD)
                    if u >= U_OGT and i % 2 == 0:
                        n = (u - U_OGT) // 2
                        pe.wait_ge(og_ready, A_HEADS + B_HEADS)
                        if n >= 2:
                            pe.wait_ge(split_lo, 8 + n - 1)
                        transpose_step(lambda b, r: g[:, r, (2 * n + b) * P:(2 * n + b + 1) * P], T0 + n % 2)
                    w_in_unit(c, i, chunk_bank(c))

            def merged_step(n, half):
                if half == 0:
                    pe.wait_ge(merged, n + 1)
                pe.wait_ge(split_lo, n * 2 + (16 + half - 1))
                transpose_step(lambda b, r: stage[:, r, (2 * half + b) * P:(2 * half + b + 1) * P], T0 + half)

            def projections(n):
                for branch in range(2):
                    for i in range(4):
                        first = isinstance(n, int)
                        if not first and branch == 0 and i >= 2:
                            merged_step(n - 1, i - 2)
                        if i == 0 and first:
                            pe.wait_ge(chunk_out, C_O - 1 + branch)
                            pe.wait_ge(split_lo, 8 + 4 * (branch + 1))
                        if i == 0 and not first:
                            pe.wait_ge(tail_out, n * 2 + (branch - 1))
                        unit(n * 8 + (U_O + 4 * branch + i), i, 8 * branch + 2 * i, ogT_hi, ogT_lo, 2 * branch,
                             i == 0, i == 3)

            projections(0)
            with pe.Fori(1, 4) as n:
                projections(n)
            for n in range(4):
                for i in range(CK):
                    if n == 0 and i in (2, 3):
                        merged_step(3, i - 2)
                    if i == 0:
                        pe.wait_ge(tail_out, 6 + n + 1)
                    if n == 0 and i in (0, 6, 7):
                        pe.wait_ge(split_lo, {0: 22, 6: 23, 7: 24}[i])
                    unit(U_W + CK * n + i, i % RING, 2 * i, hT_hi, hT_lo, 2 * (n % 2), i == 0, i == CK - 1,
                         rows_done=last_rows if n == 3 and i == CK - 1 else None)

        @block.scalar
        def _(act):
            activation = nc.scalar.activation
            act.dma_start(gain_rows[:, :], norm_gain[0].rearrange("(k p) -> k p", p=P)).then_inc(gain_landed, 16)

            def split_hi_step(t, dst, k0, bank):
                act.wait_ge(split_T, t + 1)
                activation(dst[:, bass.ds(k0, 2), :], ps[:, bank, :].rearrange("p (k s) -> p k s", k=2),
                           ACT.Copy).then_inc(split_hi, 1)

            act.wait_ge(gainT_psum, 1)
            activation(gainT[:, :], ps[:, 0, 0:KT], ACT.Copy).then_inc(gainT_ready, 1)
            act.wait_ge(gainT_ready, 1)

            def x_hi(t):
                act.wait_ge(split_T, t + 1)
                for b in range(2):
                    k = 2 * t + b
                    ins = activation(hT_hi[:, k, :], ps[:, 4 + t % 4, b * S:(b + 1) * S], ACT.Copy,
                                     scale=gainT[:, k:k + 1])
                ins.then_inc(split_hi, 1)

            def make_hi(u, slot, turn, width=CW):
                act.wait_ge(raw_landed[slot], turn * 16 + 16)
                if not isinstance(u, int) or u >= RING:
                    act.wait_ge(unit_done, u - (RING - 1))
                activation(hi[:, slot, :, 0:width], raw[:, slot, :, 0:width], ACT.Copy).then_inc(hi_ready, 1)

            def make_hi_ahead(c, i):
                width = chunk_width(c + (i + RING) // CK) if isinstance(c, int) else CW
                make_hi(c * CK + (i + RING), i % RING, c * 2 + (i // RING + 1), width)

            def chunk_to(c, dst, func=ACT.Copy, bank=None, width=CW):
                bank = chunk_bank(c) if bank is None else bank
                act.wait_ge(unit_done, c * CK + CK)
                for r in range(RT):
                    ins = activation(dst(r), ps[:, bank + r, 0:width], func, scale=rstd[:, r:r + 1])
                if isinstance(c, int) and c == C_QK - 1:
                    for r in range(RT):
                        ins = activation(kst[:, r, :], ps[:, bank + r, width:width + KIWI], func,
                                         scale=rstd[:, r:r + 1])
                ins.then_inc(chunk_out, 1)

            def index_chunk(n):
                if n > 0:
                    act.wait_ge(rope_done, n)
                width = IDX_BLOCKS[n] * P
                chunk_to(n, lambda r: stage[:, r, 0:width], width=width)

            def qk_chunk(n, bank):
                act.wait_ge(rope_done, n)
                chunk_to(n, lambda r: stage[:, r, :], bank=bank)
                act.wait_ge(chunk_out, n + 1)
                for r in range(RT):
                    for h in range(4):
                        at = slice(h * HD, (h + 1) * HD)
                        j = 4 * r + h
                        ins = activation(swapped[:, r, at], stage[:, r, at], ACT.Square,
                                         accum_out=ss_h[:, j:j + 1])
                ins.then_inc(h_squares, 1)

            def qkT_out(n):
                act.wait_ge(qk_transposed, n + 1)
                activation(qkT[:, bass.ds((n - C_QK) * 4 + QA, 4), :],
                           ps[:, T0:T0 + 2, :].rearrange("p a (b s) -> p (a b) s", b=2),
                           ACT.Copy).then_inc(qkT_ready, 1)

            def index_T_out(n):
                act.wait_ge(qk_transposed, n + 1)
                first, blocks = QI + sum(IDX_BLOCKS[:n]), IDX_BLOCKS[n]
                ins = activation(qkT[:, first:first + blocks, :],
                                 ps[:, T0:T0 + 2, :].rearrange("p a (b s) -> p (a b) s", b=2)[:, 0:blocks],
                                 ACT.Copy)
                if n == C_QK - 1:
                    ins = activation(kiT[:, :], ps[:, T0 + 1, 0:S], ACT.Copy)
                ins.then_inc(qkT_ready, 1)

            for u in range(CK):
                x_hi(u)
                make_hi(u, u % RING, u // RING, IDX_W[0])
            for i in range(4, CK):
                if i in (4, 6):
                    r = (i - 4) // 2
                    junk = qkT[:, 8 * r:8 * r + 8, :].rearrange("p a b -> p (a b)")
                    ins = activation(junk, xr[:, r, :], ACT.Square, accum_out=ss_x[:, r:r + 1])
                    if r == RT - 1:
                        ins.then_inc(x_squares, 1)
                make_hi_ahead(0, i)
            for c in range(1, C_QK + 2):
                for i in range(CK):
                    if c == 1 and i == 1:
                        act.wait_ge(reduced, 1)
                        activation(sin_t, ang, ACT.Sin).then_inc(sin_ready, 1)
                        activation(cos_t, absr, ACT.Sin, scale=-1.0, bias=HALF_PI).then_inc(sin_ready, 1)
                    if i == 0:
                        if c == 1:
                            act.wait_ge(rstd_ready, 1)
                        if c <= C_QK:
                            index_chunk(c - 1)
                        else:
                            qk_chunk(c - 1, chunk_bank(c - 1))
                    if i == 7:
                        (index_T_out if c <= C_QK else qkT_out)(c - 1)
                    make_hi_ahead(c, i)
            with act.Fori(0, 3) as pair:
                for turn in range(2):
                    c = pair * 2 + (C_QK + 2 + turn)
                    for i in range(CK):
                        if i == 0:
                            qk_chunk(c - 1, chunk_bank(C_QK + 1 + turn))
                        if i == 7:
                            qkT_out(c - 1)
                        make_hi_ahead(c, i)

            def exps(tile, buf, n):
                act.wait_ge(neg_max_ready, tile + 1)
                for t, at in enumerate((slice(0, P), slice(P, QB_COLS))):
                    j = 2 * n + t
                    ins = activation(probs[buf][:, at], masked[buf][:, at], ACT.Exp, scale=SCALE,
                                     bias=neg_max[:, j:j + 1], accum_out=sum_p[:, j:j + 1])
                ins.then_inc(probs_ready, 1)

            def probsT_out(head, buf):
                act.wait_ge(probsT_psum, head + 1)
                activation(probsT[buf], ps[:, T0 + buf, 0:QB_COLS], ACT.Copy).then_inc(probsT_ready, 1)

            for c in range(C_V, C_O):
                for i in range(CK):
                    u = c * CK + i
                    if i == 0:
                        if c == C_V:
                            qk_chunk(c - 1, chunk_bank(c - 1))
                        elif c <= C_G:
                            at = (c - 1 - C_V) * CW
                            chunk_to(c - 1, lambda r: v[:, r, at:at + CW])
                        elif c <= C_M:
                            at = (c - 1 - C_G) * CW
                            chunk_to(c - 1, lambda r: g[:, r, at:at + CW], ACT.Silu)
                        else:
                            at = (c - 1 - C_M) * CW
                            chunk_to(c - 1, lambda r: m[:, r, at:at + CW],
                                     ACT.Sigmoid if c == C_O - 1 else ACT.Copy)
                    if c == C_V and i == 7:
                        qkT_out(c - 1)
                    if C_INDEX <= c < C_INDEX + 4 and i % 2 == 0:
                        h = 4 * (c - C_INDEX) + i // 2
                        act.wait_ge(idx_scores, h + 1)
                        if h >= 2:
                            act.wait_ge(idx_added, h - 1)
                        else:
                            act.wait_ge(rope_done, C_V)
                        activation(rel[h % 2], ps[:, S0 + h % 2, 0:QB_COLS], ACT.Relu).then_inc(idx_relu, 1)
                    if U_A <= u < U_B:
                        h, step = divmod(u - U_A, 4)
                        if step == 0:
                            exps(h, h % 2, h % 2)
                        if step == 2:
                            probsT_out(h, h % 2)
                    if U_B <= u < U_OGT:
                        h, step = divmod(u - U_B, 8)
                        if u == U_B:
                            act.wait_ge(lam_sums, 1)
                            activation(lam_e, lam_s, ACT.Exp).then_inc(lam_exps, 1)
                        if step == 0:
                            for n in range(2):
                                exps(A_HEADS + 2 * h + n, n, n)
                        if step == 4:
                            probsT_out(A_HEADS + h, h % 2)
                        if step == 5:
                            act.wait_ge(heads_psum, A_HEADS + h + 1)
                            for t in range(RT):
                                ins = activation(masked[t][:, 0:2 * HD], ps[:, S0, t * 2 * HD:(t + 1) * 2 * HD],
                                                 ACT.Square, scale=inv_p[:, t:t + 1], accum_out=ss_o[:, t:t + 1])
                            ins.then_inc(o_squares, 1)
                    if u >= U_OGT and i % 2 == 0:
                        n = (u - U_OGT) // 2
                        split_hi_step(8 + n, ogT_hi, 2 * n, T0 + n % 2)
                        if n >= 1 and n <= 6:
                            act.wait_ge(chunk_out, C_M + n)
                            part = m[:, :, (n - 1) * CW:n * CW]
                            activation(part, part, ACT.Sigmoid).then_inc(gates_ready, 1)
                    make_hi_ahead(c, i)

            def merged_hi(n, half):
                t = n * 2 + half
                split_hi_step(t + 16, hT_hi, t * 2, T0 + half)

            def tail_hi_ahead(n, i):
                make_hi(n * 8 + (U_O + i + RING), i % RING, n * 2 + (U_O // RING + i // RING + 1))

            chunk_to(C_O - 1, lambda r: m[:, r, 7 * CW:8 * CW], ACT.Sigmoid)
            for i in range(8):
                tail_hi_ahead(0, i)
            with act.Fori(1, 5) as n:
                for i in range(8):
                    if i in (2, 3):
                        merged_hi(n - 1, i - 2)
                    tail_hi_ahead(n, i)
            for n in range(5, 8):
                for i in range(8):
                    if U_O + 8 * n + i + RING < U_END:
                        tail_hi_ahead(n, i)

        @block.vector
        def _(dve):
            tt, stt, ts = nc.vector.tensor_tensor, nc.vector.scalar_tensor_tensor, nc.vector.tensor_scalar
            wrote = [0]

            def mark(ins):
                ins.then_inc(dve_wrote, 1)
                wrote[0] = wrote[0] + 1

            def settle():
                dve.wait_ge(dve_wrote, wrote[0])

            def split_lo_step(t, dst, src_hi, k0, bank):
                dve.wait_ge(split_hi, t + 1)
                tt(dst[:, bass.ds(k0, 2), :], ps[:, bank, :].rearrange("p (k s) -> p k s", k=2),
                   src_hi[:, bass.ds(k0, 2), :].bitcast(F32), ALU.subtract).then_inc(split_lo, 1)

            def x_lo(t):
                dve.wait_ge(split_hi, t + 1)
                for b in range(2):
                    k = 2 * t + b
                    ins = stt(hT_lo[:, k, :], ps[:, 4 + t % 4, b * S:(b + 1) * S], gainT[:, k:k + 1],
                              hT_hi[:, k, :].bitcast(F32), ALU.mult, ALU.subtract)
                ins.then_inc(split_lo, 1)

            def make_lo(u, slot, width=CW):
                dve.wait_ge(hi_ready, u + 1)
                tt(lo[:, slot, :, 0:width], raw[:, slot, :, 0:width], hi[:, slot, :, 0:width].bitcast(F32),
                   ALU.subtract).then_inc(lo_ready, 1)

            def make_lo_ahead(c, i):
                width = chunk_width(c + (i + RING) // CK) if isinstance(c, int) else CW
                make_lo(c * CK + (i + RING), i % RING, width)

            def rope_products(n, width, cos_of, sin_of, rows, cols=CW):
                heads, hw = cols // width, width // 2
                src, cos_out, sin_out = (t[:, :, 0:cols].rearrange("p r (h d) -> p r h d", d=width)
                                         for t in (stage, roped, swapped))
                if 0 in rows and not (isinstance(n, int) and n == 0):
                    dve.wait_ge(qk_transposed, n)
                for r in rows:
                    c_tab = cos_of(r).unsqueeze(1).to_broadcast([P, heads, width])
                    mark(tt(cos_out[:, r], src[:, r], c_tab, ALU.mult))
                    for b in range(2):
                        half_b, other = slice(b * hw, (b + 1) * hw), slice((1 - b) * hw, (2 - b) * hw)
                        s_tab = sin_of(r)[:, half_b].unsqueeze(1).to_broadcast([P, heads, hw])
                        mark(tt(sin_out[:, r, :, half_b], src[:, r, :, other], s_tab, ALU.mult))

            def rope_sum(cols=CW):
                settle()
                tt(roped[:, :, 0:cols], roped[:, :, 0:cols], swapped[:, :, 0:cols], ALU.add).then_inc(rope_done, 1)

            def norm_rope(n, i_tab, step):
                if step == 0:
                    if isinstance(n, int) and n == C_QK:
                        dve.wait_ge(tables_ready, 4 * RT + 1)
                    dve.wait_ge(r_h_ready, n - (C_QK - 1))
                    src = stage[:, :, :].rearrange("p r (h d) -> p (r h) d", d=HD)
                    mark(tt(src, src, r_h.unsqueeze(2).to_broadcast([P, 8, HD]), ALU.mult))
                elif step == 1:
                    settle()
                    rope_products(n, HD, lambda r: tab_c[:, bass.ds(i_tab, 1), r, :].squeeze(1),
                                  lambda r: tab_s[:, bass.ds(i_tab, 1), r, :].squeeze(1), range(RT))
                else:
                    rope_sum()

            def index_rope(n, step):
                if step == 0:
                    dve.wait_ge(index_tables_ready, 4 * RT)
                    dve.wait_ge(chunk_out, n + 1)
                    rope_products(n, IDX_DIM, lambda r: tab_ci[:, r, :], lambda r: tab_si[:, r, :], range(RT),
                                  IDX_BLOCKS[n] * P)
                if n == C_QK - 1 and step == 0:
                    mark(tt(k_cos, kst[:, :, 0:IDX_DIM], tab_ci, ALU.mult))
                    for b in range(2):
                        half_b, other = slice(b * 32, b * 32 + 32), slice(32 - b * 32, 64 - b * 32)
                        mark(tt(k_swap[:, :, half_b], kst[:, :, other], tab_si[:, :, half_b], ALU.mult))
                    mark(ts(w_idx[:, :, :], kst[:, :, IDX_DIM:KIWI], IDX_SCALE, None, ALU.mult))
                if n == C_QK - 1 and step == 1:
                    settle()
                    for b in range(2):
                        mark(tt(kr[:, :, b * IDX_DIM:(b + 1) * IDX_DIM], k_cos, k_swap, ALU.add))
                if step == 1:
                    rope_sum(IDX_BLOCKS[n] * P)

            for u in range(CK):
                x_lo(u)
                make_lo(u, u % RING, IDX_W[0])
            for i in range(4, CK):
                make_lo_ahead(0, i)
            for c in range(1, C_QK + 2):
                for i in range(CK):
                    if c == 4 and i == 4:
                        dve.wait_ge(consts_landed, 11 * 16)
                        mark(tt(lam_prod[:, 0], lams[:, 0], lams[:, 1], ALU.mult))
                        mark(tt(lam_prod[:, 1], lams[:, 2], lams[:, 3], ALU.mult))
                        settle()
                        nc.vector.reduce_sum(lam_s, lam_prod, axis=mybir.AxisListType.X).then_inc(lam_sums, 1)
                    start = 3 if c == 1 else 1
                    if c <= C_QK and i in (start, start + 1):
                        index_rope(c - 1, i - start)
                    if c == C_QK + 1 and 1 <= i <= 3:
                        norm_rope(c - 1, 0, i - 1)
                    make_lo_ahead(c, i)
            before = wrote[0]
            for_each = 2 * (1 + 6)
            with dve.Fori(0, 3) as pair:
                wrote[0] = pair * for_each + before
                for turn in range(2):
                    c = pair * 2 + (C_QK + 2 + turn)
                    for i in range(CK):
                        if 1 <= i <= 3:
                            norm_rope(c - 1, pair + turn, i - 1)
                        make_lo_ahead(c, i)
            wrote[0] = before + 3 * for_each

            def masked_max(buf, bank, bias, n, tile):
                dve.wait_ge(scores, tile + 1)
                for t, at in enumerate((slice(0, P), slice(P, QB_COLS))):
                    j = 2 * n + t
                    mark(nc.vector.tensor_tensor_reduce(
                        out=masked[buf][:, at], in0=ps[:, bank, at], in1=bias[:, at], scale=1.0, scalar=MARK,
                        op0=ALU.add, op1=ALU.max, accum_out=max_s[:, j:j + 1]))
                settle()
                ts(neg_max[:, 2 * n:2 * n + 2], max_s[:, 2 * n:2 * n + 2], -SCALE, None,
                   ALU.mult).then_inc(neg_max_ready, 1)

            def topk_round():
                tiles = (slice(0, P), slice(P, QB_COLS))
                settle()
                for t, at in enumerate(tiles):
                    mark(nc.vector.max(top8[:, t], score[:, at]))
                settle()
                for t, at in enumerate(tiles):
                    mark(nc.vector.match_replace(score[:, at], top8[:, t], score[:, at], MARK))

            for c in range(C_V, C_O):
                for i in range(CK):
                    u = c * CK + i
                    if c == C_V and 1 <= i <= 3:
                        norm_rope(c - 1, 3, i - 1)
                    if C_INDEX <= c < C_INDEX + 4 and i % 2 == 0:
                        h = 4 * (c - C_INDEX) + i // 2
                        if h == 0:
                            dve.wait_ge(causal_ready, 1)
                        dve.wait_ge(idx_relu, h + 1)
                        settle()
                        for t, at in enumerate((slice(0, P), slice(P, QB_COLS))):
                            ins = stt(score[:, at], rel[h % 2][:, at], w_idx[:, t, h:h + 1],
                                      (bias_b if h == 0 else score)[:, at], ALU.mult, ALU.add)
                            if t == 0:
                                mark(ins)
                        ins.then_inc(idx_added, 1)
                        dve.wait_ge(idx_added, h + 1)
                    if c == U_TOPK // CK:
                        topk_round()
                    if u == U_A - 1:
                        settle()
                        mark(ts(bias_a[:, :], score[:, :], 0.5 * MARK, NEG, ALU.is_gt, ALU.mult))
                        settle()
                        mark(tt(bias_a[:, :], bias_a[:, :], bias_b[:, :], ALU.add))
                        settle()
                    if U_A <= u < U_B:
                        h, step = divmod(u - U_A, 4)
                        n = h % 2
                        if step == 0:
                            masked_max(n, S0 + n, bias_a, n, h)
                        if step == 3:
                            dve.wait_ge(probs_ready, h + 1)
                            mark(nc.vector.reciprocal(inv_p[:, 2 * n:2 * n + 2], sum_p[:, 2 * n:2 * n + 2]))
                            dve.wait_ge(heads_psum, h + 1)
                            dve.wait_ge(chunk_out, C_G + 2)
                            settle()
                            for t in range(RT):
                                part = g[:, t, h * HD:(h + 1) * HD]
                                ins = stt(part, ps[:, S0 + n, t * HD:(t + 1) * HD], inv_p[:, 2 * n + t:2 * n + t + 1],
                                          part, ALU.mult, ALU.mult)
                            ins.then_inc(og_ready, 1)
                    if c == C_M and i in (1, 2):
                        r = i - 1
                        if r == 0:
                            dve.wait_ge(chunk_out, C_M)
                        part = g[:, r, A_W:2 * A_W].rearrange("p (h d) -> p h d", d=2 * HD)
                        mark(tt(part, part, sub_gain[:, :].unsqueeze(1).to_broadcast([P, B_HEADS, 2 * HD]), ALU.mult))
                    if U_B <= u < U_OGT:
                        h, step = divmod(u - U_B, 8)
                        if step == 0:
                            for n in range(2):
                                masked_max(n, S0 + n, bias_b, n, A_HEADS + 2 * h + n)
                        if step == 2:
                            dve.wait_ge(probs_ready, A_HEADS + 2 * h + 2)
                            mark(nc.vector.reciprocal(inv_p, sum_p))
                            if h == 0:
                                dve.wait_ge(lam_exps, 1)
                                mark(stt(neg_lam, lam_e[:, 1:2], -LAMBDA_INIT, lam_e[:, 0:1],
                                         ALU.add, ALU.subtract))
                            settle()
                            mark(stt(mix, sum_p[:, 0:2], neg_lam, inv_p[:, 2:4], ALU.mult, ALU.mult))
                            settle()
                            for t, at in enumerate((slice(0, P), slice(P, QB_COLS))):
                                ins = stt(probs[0][:, at], probs[1][:, at], mix[:, t:t + 1], probs[0][:, at],
                                          ALU.mult, ALU.add)
                            ins.then_inc(mixed, 1)
                        if step == 6:
                            dve.wait_ge(r_o_ready, h + 1)
                            mark(tt(f_o, r_o, inv_p[:, 0:2], ALU.mult))
                            settle()
                            for t in range(RT):
                                at = A_W + h * 2 * HD
                                part = g[:, t, at:at + 2 * HD]
                                ins = stt(part, ps[:, S0, t * 2 * HD:(t + 1) * 2 * HD], f_o[:, t:t + 1], part,
                                          ALU.mult, ALU.mult)
                            ins.then_inc(og_ready, 1)
                    if u >= U_OGT and i % 2 == 0:
                        n = (u - U_OGT) // 2
                        split_lo_step(8 + n, ogT_lo, ogT_hi, 2 * n, T0 + n % 2)
                    make_lo_ahead(c, i)

            def add_residual(u, n):
                dve.wait_ge(unit_done, u)
                if n == 0:
                    dve.wait_ge(res_landed, 16)
                part = g[:, :, n * CW:(n + 1) * CW]
                bank = 2 * (n % 2)
                tt(part, ps[:, bank:bank + 2, :], part, ALU.add).then_inc(tail_out, 1)

            def gate_a(n):
                dve.wait_ge(unit_done, n * 8 + (U_O + 4))
                part = m[:, :, bass.ds(n * CW, CW)]
                tt(part, ps[:, 0:2, :], part, ALU.mult).then_inc(tail_out, 1)

            def gate_b_and_merge(n):
                dve.wait_ge(unit_done, n * 8 + (U_O + 8))
                a_part, b_part = (m[:, :, bass.ds(n * CW + b * D, CW)] for b in range(2))
                tt(b_part, ps[:, 2:4, :], b_part, ALU.mult).then_inc(tail_out, 1)
                dve.wait_ge(tail_out, n * 2 + 2)
                dve.wait_ge(split_T, n * 2 + 16)
                tt(stage[:, :, :], a_part, b_part, ALU.add).then_inc(merged, 1)

            def merged_lo(n, half):
                t = n * 2 + half
                split_lo_step(t + 16, hT_lo, hT_hi, t * 2, T0 + half)

            def tail_lo_ahead(n, i):
                make_lo(n * 8 + (U_O + i + RING), i % RING)

            for i in range(8):
                if i == 4:
                    dve.wait_ge(gates_ready, 6)
                    dve.wait_ge(chunk_out, C_O)
                    gate_a(0)
                tail_lo_ahead(0, i)
            with dve.Fori(1, 4) as n:
                for i in range(8):
                    if i == 0:
                        gate_b_and_merge(n - 1)
                    if i in (2, 3):
                        merged_lo(n - 1, i - 2)
                    if i == 4:
                        gate_a(n)
                    tail_lo_ahead(n, i)
            for n in range(4, 8):
                for i in range(8):
                    u = U_O + 8 * n + i
                    if n == 4 and i == 0:
                        gate_b_and_merge(3)
                    if n == 4 and i in (2, 3):
                        merged_lo(3, i - 2)
                    if n >= 5 and i == 0:
                        add_residual(u, n - 5)
                    if u + RING < U_END:
                        tail_lo_ahead(n, i)
            for r in range(RT):
                if r == 0:
                    dve.wait_ge(last_rows, 1)
                else:
                    dve.wait_ge(unit_done, U_END)
                part = g[:, r, 3 * CW:4 * CW]
                tt(part, ps[:, 2 + r, :], part, ALU.add).then_inc(tail_out, 1)


_INS = ["x", "positions", "inv_freq", "norm_gain", "w_in", "a_q_gain", "a_k_gain", "b_q_gain", "b_k_gain",
        "lambda_q1", "lambda_k1", "lambda_q2", "lambda_k2", "b_subln_gain", "w_o_a", "w_o_b", "w_out"]


def kernel(**inputs):
    import numpy as _np
    import concourse.bacc as _bacc
    from concourse import mybir as _mybir
    from concourse.bass_utils import run_bass_kernel_spmd as _run

    exponents = _np.arange(0, HD, 2, dtype=_np.float32) / _np.float32(HD)
    freqs = (_np.float32(10000.0) ** -exponents).astype(_np.float32)[None]

    nc = _bacc.Bacc("TRN2", target_bir_lowering=False, num_devices=1)
    arrays, args = {}, []
    for name in _INS:
        a = freqs if name == "inv_freq" else _np.ascontiguousarray(inputs[name])
        arrays[f"in_{name}"] = a
        args.append(nc.dram_tensor(f"in_{name}", a.shape, _mybir.dt.from_np(a.dtype), kind="ExternalInput").ap())
    args.append(nc.dram_tensor("out_0", (1, S, D), _mybir.dt.from_np(_np.dtype("float32")),
                               kind="ExternalOutput").ap())
    build_layer(nc, *args)
    return _run(nc, [arrays], core_ids=[0]).results[0]["out_0"]
```
